# Optimizing a Trainium2 kernel written in Bass

```python
import math
import jax, jax.numpy as jnp
from jax import lax
import numpy as np

D_MODEL = 1024
BATCH = 1
SEQ = 512
DEPTH = 2

N_MIXERS = 2
EXPAND = 2
D_INNER = EXPAND * D_MODEL
EPS = 1e-6

HG_DK = 128
HG_HEADS = D_INNER // HG_DK
HG_DV = D_INNER // HG_HEADS
HG_CHUNK = 32

ATT_HEAD_DIM = 128
ATT_HEADS = D_INNER // ATT_HEAD_DIM
DILATED_GROUPS = ((128, 1), (512, 4), (2048, 16))
N_GROUPS = len(DILATED_GROUPS)
ATT_BLOCK = 128
N_BUCKETS = 32
MAX_DISTANCE = 2048

N_A = (DEPTH + 1) // 2
N_B = DEPTH // 2
ATT_IN_COLS = (3 * N_GROUPS + 1) * D_INNER
HG_IN_COLS = 4 * D_INNER

kernel_name = "hgrn2_dilated_swa_interleaved_hybrid"

def rmsnorm(x, g):
    xf = x.astype(jnp.float32)
    y = xf * lax.rsqrt(jnp.mean(xf * xf, axis=-1, keepdims=True) + EPS)
    return (y * g.astype(jnp.float32)).astype(x.dtype)

def proj_cols(u, w, start, width):
    return u @ w[:, start:start + width]

def hgrn2_mixer(u, w_in, lb, norm_g, w_out):
    B, S, _ = u.shape
    W = D_INNER
    q = proj_cols(u, w_in, 0, W)
    f_pre = proj_cols(u, w_in, W, W)
    i_in = proj_cols(u, w_in, 2 * W, W)
    gate = proj_cols(u, w_in, 3 * W, W)

    f = lb + (1.0 - lb) * jax.nn.sigmoid(f_pre.astype(jnp.float32))
    log_f = jnp.log(f)
    k = 1.0 - f
    n_chunks = S // HG_CHUNK

    def chunks(t):
        t = t.astype(jnp.float32).reshape(B, n_chunks, HG_CHUNK, HG_HEADS, -1)
        return t.transpose(1, 0, 3, 2, 4)

    causal = jnp.tril(jnp.ones((HG_CHUNK, HG_CHUNK), dtype=bool))

    def step(state, xs):
        q_c, k_c, lf_c, v_c = xs
        b = jnp.cumsum(lf_c, axis=2)
        b_last = b[:, :, -1:, :]
        q_dec = q_c * jnp.exp(b)
        scores = jnp.einsum('bhcd,bhsd->bhcs', q_dec, k_c * jnp.exp(-b))
        scores = jnp.where(causal, scores, 0.0)
        o = (jnp.einsum('bhcs,bhse->bhce', scores, v_c)
             + jnp.einsum('bhcd,bhde->bhce', q_dec, state))
        state = (jnp.exp(b_last[:, :, 0, :])[..., None] * state
                 + jnp.einsum('bhcd,bhce->bhde', k_c * jnp.exp(b_last - b), v_c))
        return state, o

    s0 = jnp.zeros((B, HG_HEADS, HG_DK, HG_DV), jnp.float32)
    _, o = lax.scan(step, s0, (chunks(q), chunks(k), chunks(log_f), chunks(i_in)))
    o = o.transpose(1, 0, 3, 2, 4).reshape(B, S, HG_HEADS, HG_DV)
    o = o * lax.rsqrt(jnp.mean(o * o, axis=-1, keepdims=True) + EPS)
    o = o.reshape(B, S, D_INNER) * norm_g.astype(jnp.float32)
    y = o * jax.nn.silu(gate.astype(jnp.float32))
    return y.astype(u.dtype) @ w_out

def t5_bucket(dist):
    max_exact = N_BUCKETS // 2
    df = jnp.maximum(dist, 1).astype(jnp.float32)
    large = max_exact + (jnp.log(df / max_exact) / math.log(MAX_DISTANCE / max_exact)
                         * (N_BUCKETS - max_exact)).astype(jnp.int32)
    large = jnp.minimum(large, N_BUCKETS - 1)
    return jnp.where(dist < max_exact, dist, large)

def dilated_group(q, k, v, bias_table, window, dilation):
    B, S, H, E = q.shape
    d = dilation
    L = S // d
    n_blk = -(-L // ATT_BLOCK)
    Lp = n_blk * ATT_BLOCK
    sub_window = window // d

    def by_residue(t):
        t = t.reshape(B, L, d, H, E).transpose(0, 2, 1, 3, 4)
        return jnp.pad(t, ((0, 0), (0, 0), (0, Lp - L), (0, 0), (0, 0)))

    def banded(t):
        t = jnp.pad(t, ((0, 0), (0, 0), (ATT_BLOCK, 0), (0, 0), (0, 0)))
        t = t.reshape(B, d, n_blk + 1, ATT_BLOCK, H, E)
        return jnp.concatenate([t[:, :, :-1], t[:, :, 1:]], axis=3)

    qb = by_residue(q).reshape(B, d, n_blk, ATT_BLOCK, H, E)
    kb = banded(by_residue(k))
    vb = banded(by_residue(v))

    a = jnp.arange(ATT_BLOCK)[:, None]
    c = jnp.arange(2 * ATT_BLOCK)[None, :]
    rel = ATT_BLOCK + a - c
    band = (rel >= 0) & (rel <= sub_window)
    kpos = (jnp.arange(n_blk)[:, None, None] - 1) * ATT_BLOCK + c[None]
    mask = band[None] & (kpos >= 0)
    bucket = t5_bucket(jnp.maximum(rel, 0) * d)
    bias = bias_table[bucket].astype(jnp.float32).transpose(2, 0, 1)

    s = jnp.einsum('brnqhe,brnkhe->brnhqk', qb, kb,
                   preferred_element_type=jnp.float32) * (E ** -0.5) + bias
    s = jnp.where(mask[None, None, :, None], s, -1e30)
    m = jnp.max(s, axis=-1, keepdims=True)
    p = jnp.exp(s - m)
    den = jnp.sum(p, axis=-1)
    o = jnp.einsum('brnhqk,brnkhe->brnqhe', p, vb.astype(jnp.float32))
    o = o / den.transpose(0, 1, 2, 4, 3)[..., None]
    lse = (m[..., 0] + jnp.log(den)).transpose(0, 1, 2, 4, 3)

    o = o.reshape(B, d, Lp, H, E)[:, :, :L].transpose(0, 2, 1, 3, 4).reshape(B, S, H, E)
    lse = lse.reshape(B, d, Lp, H)[:, :, :L].transpose(0, 2, 1, 3).reshape(B, S, H)
    return o, lse

def dilated_attention_mixer(u, w_in, rel_bias, w_out):
    B, S, _ = u.shape
    W = D_INNER
    outs, lses = [], []
    for g, (window, dilation) in enumerate(DILATED_GROUPS):
        base = 3 * g * W
        q = proj_cols(u, w_in, base, W).reshape(B, S, ATT_HEADS, ATT_HEAD_DIM)
        k = proj_cols(u, w_in, base + W, W).reshape(B, S, ATT_HEADS, ATT_HEAD_DIM)
        v = proj_cols(u, w_in, base + 2 * W, W).reshape(B, S, ATT_HEADS, ATT_HEAD_DIM)
        table = rel_bias[:, g * ATT_HEADS:(g + 1) * ATT_HEADS]
        o, lse = dilated_group(q, k, v, table, window, dilation)
        outs.append(o)
        lses.append(lse)
    wts = jax.nn.softmax(jnp.stack(lses, axis=0), axis=0)
    o = jnp.einsum('gbsh,gbshe->bshe', wts, jnp.stack(outs, axis=0)).reshape(B, S, W)
    gate = proj_cols(u, w_in, 3 * N_GROUPS * W, W)
    y = o * jax.nn.silu(gate.astype(jnp.float32))
    return y.astype(u.dtype) @ w_out

def setup_inputs(seed: int = 0) -> dict:
    key = jax.random.key(seed)
    ks = jax.random.split(key, 10)
    f32 = jnp.float32
    x = jax.random.normal(ks[0], (BATCH, SEQ, D_MODEL), f32)
    ln_g = 1.0 + 0.02 * jax.random.normal(ks[1], (DEPTH, D_MODEL), f32)
    hg_w_in = jax.random.normal(ks[2], (N_A, D_MODEL, HG_IN_COLS), f32) * D_MODEL ** -0.5
    hg_lb_logits = 0.1 * jax.random.normal(ks[3], (DEPTH + 1, D_INNER), f32)
    hg_norm_g = 1.0 + 0.02 * jax.random.normal(ks[4], (N_A, D_INNER), f32)
    hg_w_out = jax.random.normal(ks[5], (N_A, D_INNER, D_MODEL), f32) * D_INNER ** -0.5
    att_w_in = jax.random.normal(ks[6], (N_B, D_MODEL, ATT_IN_COLS), f32) * D_MODEL ** -0.5
    att_w_out = jax.random.normal(ks[7], (N_B, D_INNER, D_MODEL), f32) * D_INNER ** -0.5
    rel_bias = 0.2 * jax.random.normal(ks[8], (N_BUCKETS, N_GROUPS * ATT_HEADS), f32)
    final_g = 1.0 + 0.02 * jax.random.normal(ks[9], (D_MODEL,), f32)
    return {"x": x, "ln_g": ln_g, "hg_w_in": hg_w_in, "hg_lb_logits": hg_lb_logits,
            "hg_norm_g": hg_norm_g, "hg_w_out": hg_w_out, "att_w_in": att_w_in,
            "att_w_out": att_w_out, "rel_bias": rel_bias, "final_g": final_g}

def reference(x, ln_g, hg_w_in, hg_lb_logits, hg_norm_g, hg_w_out, att_w_in, att_w_out,
              rel_bias, final_g):
    lower_bounds = jnp.cumsum(jax.nn.softmax(hg_lb_logits.astype(jnp.float32), axis=0), axis=0)
    h = x
    for i in range(DEPTH):
        u = rmsnorm(h, ln_g[i])
        j = i // N_MIXERS
        if i % N_MIXERS == 0:
            y = hgrn2_mixer(u, hg_w_in[j], lower_bounds[i], hg_norm_g[j], hg_w_out[j])
        else:
            y = dilated_attention_mixer(u, att_w_in[j], rel_bias, att_w_out[j])
        h = h + y.astype(h.dtype)
    return rmsnorm(h, final_g)


_drawn_inputs = setup_inputs


def setup_inputs(seed=0):
    import zlib

    import numpy as np

    out = dict(_drawn_inputs(seed))
    spreads = {}
    factors = {}
    for name, (base, spread) in spreads.items():
        noise = np.random.default_rng([zlib.crc32(name.encode()), seed]).standard_normal(out[name].shape)
        drawn = base * np.exp(spread * noise) if base else spread * noise
        out[name] = __import__('jax').numpy.asarray(drawn.astype(out[name].dtype))
    for name, factor in factors.items():
        out[name] = (out[name] * factor).astype(out[name].dtype)
    return out
```

```python
from contextlib import ExitStack

import numpy as np

import concourse.bass as bass
from concourse import mybir

F32 = mybir.dt.float32
F32R = mybir.dt.float32r
ALU = mybir.AluOpType
ACT = mybir.ActivationFunctionType
AX = mybir.AxisListType
ds = bass.ds

P = 128
S = 512
D = 1024
W = 2048
KT = D // P
H = W // P
HQ = 4
NQ = H // HQ
ST = S // P
CH = 32
NC = P // CH
GROUPS = 3
RES = 4
BUCKETS = 32
EPS = 1e-6
QSCALE = float(P) ** -0.5
MASKED = -1e30
SLOTS = 4
TW = 1024
BANKS = 3
EXT = 384


class Layer:

    def __init__(self, tile0, event0, value0, per_head, groups):
        self.value0 = value0
        self.per_head, self.groups = per_head, groups
        self.tile0, self.event0 = tile0, event0
        self.pro = 4 * groups
        self.heads = HQ * per_head
        self.T = self.heads + self.pro + 4
        self.EV = self.heads + self.pro + 8
        assert self.T % SLOTS == 0 and self.EV % BANKS == 0 and tile0 % SLOTS == 0
        self.tiles = self.pro + (NQ - 1) * self.T + self.heads + 4
        self.events = self.pro + (NQ - 1) * self.EV + self.heads + 8

    def tile(self, q, n):
        first = self.tile0 + n + (0 if q is None else self.pro)
        off = 0 if q is None else q * self.T
        turn = 0 if q is None else q * (self.T // SLOTS)
        return off + first, first % SLOTS, turn + first // SLOTS

    def event(self, q, n):
        first = self.event0 + n + (0 if q is None else self.pro)
        off = 0 if q is None else q * self.EV
        turn = 0 if q is None else q * (self.EV // BANKS)
        return off + first, first % BANKS, turn + first // BANKS

    def kind(self, n, last):
        if n < self.heads:
            return "head", n // self.per_head, n % self.per_head
        n -= self.heads
        if not last:
            if n < self.pro:
                return "value", n // 4, n % 4
            n -= self.pro
        return "out", 0, n

    def quad_tiles(self, last):
        return self.heads + 4 + (0 if last else self.pro)


HG = Layer(0, 0, 0, 3, 1)
AT = Layer(HG.tiles, HG.events, 3 * NQ * HG.groups, 7, GROUPS)
HG_COLS = (1 * W, 0 * W, 3 * W)
AT_COLS = (0, W, 3 * W, 4 * W, 6 * W, 7 * W, 9 * W)
HG_VALUE = (2 * W,)
AT_VALUE = (2 * W, 5 * W, 8 * W)
F_, Q_, G_ = 0, 1, 2
Q0, K0, Q1, K1, Q2, K2, GA = range(7)
LINKS_HG = 4 * 15
LINKS_AT = 4 * 9
TILES = [(0, 0)] + [(b, c) for b in range(1, ST) for c in (b - 1, b)] + [(r, g) for r in range(RES) for g in (1, 2)]
NATURAL = 2 * ST - 1
BATCHES = [range(i, min(i + 4, len(TILES))) for i in range(0, len(TILES), 4)]


def program(nc, x, ln_g, hg_w_in, hg_lb, hg_norm, hg_w_out, at_w_in, at_w_out, rel_bias, final_g,
            consts, onehot, relmask, out):
    ctx = ExitStack()
    with ctx:
        def sb(name, shape, dt=F32):
            return ctx.enter_context(nc.sbuf_tensor(name, shape, dt))

        def sem(name):
            return ctx.enter_context(nc.semaphore(name))

        x_v = x.rearrange("(t p) d -> t p d", p=P)
        out_v = out.rearrange("(t p) d -> t p d", p=P)
        w_in = {HG: hg_w_in.rearrange("(k p) n -> p k n", p=P), AT: at_w_in.rearrange("(k p) n -> p k n", p=P)}
        w_out = {HG: hg_w_out.rearrange("(k p) n -> p k n", p=P), AT: at_w_out.rearrange("(k p) n -> p k n", p=P)}
        ext_dram = nc.dram_tensor("ext_rows", [GROUPS, H, EXT], F32, kind="Internal").ap()
        bias_dram = nc.dram_tensor("bias_tiles", [H, P, 4 * P], F32, kind="Internal").ap()
        nat_dram = nc.dram_tensor("natural_stats", [2, S], F32, kind="Internal").ap()
        res_dram = nc.dram_tensor("residue_stats", [2, S], F32, kind="Internal").ap()

        ident = sb("ident", [P, P])
        causal = sb("causal", [P, P])
        restart = sb("restart", [P, S])
        ones = sb("ones", [P, P])
        param = sb("param", [P, 80])
        lb = sb("lb", [P, H])
        oml = sb("oml", [P, H])
        eps = sb("eps", [P, 1])
        u = {"hi": sb("u_hi", [P, KT, S], F32R), "lo": sb("u_lo", [P, KT, S], F32R)}
        hT = sb("hT", [P, KT, S])
        raw = sb("raw", [P, SLOTS, TW])
        w = {"hi": sb("w_hi", [P, SLOTS, TW], F32R), "lo": sb("w_lo", [P, SLOTS, TW], F32R)}
        y = {"hi": sb("y_hi", [P, HQ, S], F32R), "lo": sb("y_lo", [P, HQ, S], F32R)}
        v_sb = [sb(f"v{g}", [P, ST, S]) for g in range(GROUPS)]
        y_f = sb("y_f", [P, S])
        eg = sb("eg", [P, S])
        sg = sb("sg", [P, S])
        tmp = sb("tmp", [P, 2, S])
        rstd = sb("rstd", [P, S])
        rows = sb("rows", [P, 10, S])
        ef, fg, kk, lnf, bb, eb, enb, qd, qs, sT = [rows[:, i, :] for i in range(10)]
        keys = sb("keys", [P, ST, NC + 1, P])
        dec = sb("dec", [P, ST, NC + 1])
        kT = sb("kT", [P, ST - 1, P])
        state = sb("state", [P, ST - 1, P])
        qk = sb("qk", [P, 6, S])
        flat_rows = rows[:, :, :].rearrange("p a b -> p (a b)")
        pT = flat_rows[:, 0:len(TILES) * P].rearrange("p (a b) -> p a b", b=P)
        probs = flat_rows[:, 4 * S:8 * S].rearrange("p (a b) -> p a b", b=2 * P)
        bias_n = sb("bias_n", [P, 2 * P])
        bias_r = sb("bias_r", [P, 2, P])
        stat = sb("stat", [P, 2, 2, ST])
        stat_o = sb("stat_o", [P, 2, 2, ST])
        negm = sb("negm", [P, 2 * ST])
        both = sb("both", [P, 2, 2, ST])
        merge = sb("merge", [P, 2, 2, ST])
        share = sb("share", [P, 2, ST])
        cols = sb("cols", [P, 16])
        x_sb = qk
        prow = probs[:, :, :].rearrange("p a b -> p (a b)")
        onehot_sb = pT[:, :, :].rearrange("p a b -> p (a b)")[0:BUCKETS, 0:GROUPS * EXT]
        relmask_sb = keys[:, :, :, :].rearrange("p a b c -> p (a b c)")[0:H, 0:GROUPS * EXT]
        ext_sb = keys[:, :, :, :].rearrange("p a b c -> p (a b c)")[0:H, GROUPS * EXT:2 * GROUPS * EXT]
        relb_sb = bias_n[0:BUCKETS, 0:GROUPS * H]
        fin = qk[:, :, :].rearrange("p a b -> p (a b)")
        fg_bc = v_sb[0][:, 0:2, :].rearrange("p a b -> p (a b)")

        proj = [ctx.enter_context(nc.psum_tensor(f"proj{i}", [P, S], F32)) for i in range(BANKS)]
        inner = [ctx.enter_context(nc.psum_tensor(f"inner{i}", [P, S], F32)) for i in range(5)]
        p_sc, p_kT, p_U, p_O, p_ss = inner
        p_S = inner[0:2]
        p_T = (inner[2], inner[4])

        x_loaded = [sem(f"x_loaded{i}") for i in range(2)]
        const_loaded = [sem(f"const_loaded{i}") for i in range(8)]
        loaded = [sem(f"loaded{i}") for i in range(SLOTS)]
        bank_free = [sem(f"bank_free{i}") for i in range(BANKS)]
        (ones_ready, eps_ready, x_T, x_copied, param_T, param_ready, lb_step, lb_exp, ext_done, ext_ready, ext_stored, bias_stored, sp_met, pool_met,
         hi_ready, w_ready, value_tile_done, proj_done,
         sq_ready, sq_used, ss_done, rstd_step, rstd_ready, u_made, u_hi_ready, u_ready,
         link_hg, link_at, f_ready, lnf_ready, b_ready, eb_ready, expg_ready,
         q_ready, keys_ready, scores_done, kT_done, kT_ready, U_done, sT_ready, state_ready,
         O_done, osq_ready, osum_done, orstd_step, orstd_ready, y_made, y_hi_ready, y_ready,
         nat_done, res_done, nat_logits, res_logits, nat_probs, res_probs, bias_used,
         stat_a, stat_b, stat_back, merge_in, merge_exp, scaled, T_done, T_even, T_odd,
         fin_T, fin_copied, fin_sq, fin_step, fin_rstd, fin_ready) = [sem(n) for n in (
             "ones_ready eps_ready x_T x_copied param_T param_ready lb_step lb_exp ext_done ext_ready ext_stored bias_stored sp_met pool_met "
             "hi_ready w_ready value_tile_done proj_done "
             "sq_ready sq_used ss_done rstd_step rstd_ready u_made u_hi_ready u_ready "
             "link_hg link_at f_ready lnf_ready b_ready eb_ready expg_ready "
             "q_ready keys_ready scores_done kT_done kT_ready U_done sT_ready state_ready "
             "O_done osq_ready osum_done orstd_step orstd_ready y_made y_hi_ready y_ready "
             "nat_done res_done nat_logits res_logits nat_probs res_probs bias_used "
             "stat_a stat_b stat_back merge_in merge_exp scaled T_done T_even T_odd "
             "fin_T fin_copied fin_sq fin_step fin_rstd fin_ready").split()]
        bias_loaded = [sem("bias_n_loaded"), sem("bias_r_loaded")]
        out_stored = [sem(f"out_stored{i}") for i in range(2)]

        def head(q, h):
            return q * HQ + h

        def quads(eng, body):
            with eng.Fori(0, NQ - 1) as q:
                body(q, False)
            body(NQ - 1, True)

        def wait_turn(eng, met, signal, value):
            eng.wait_ge(signal, value)
            eng.sem_inc(met, 1)

        def wait_emptied(eng, layer, q, e):
            _, bank, before = layer.event(q, e)
            eng.wait_ge(bank_free[bank], before + 1)

        def wait_tile_done(eng, layer, q, n, last):
            if q is None:
                kind, group, part = "value", n // 4, n % 4
                count, e = layer.value0 + 3 * group + part + 1, 4 * group + 3
            else:
                kind, group, part = layer.kind(n, last)
                count = layer.value0 + 3 * layer.groups * (q + 1) + 3 * group + part + 1
                e = {"head": n, "value": layer.heads + 4 * group + 3,
                     "out": layer.heads + (0 if last else layer.pro) + 2 * part + 1}[kind]
            if kind == "value" and part < 3:
                eng.wait_ge(value_tile_done, count)
            else:
                eng.wait_ge(proj_done, layer.event(q, e)[0] + 1)

        block = ctx.enter_context(nc.Block())

        @block.sync
        def _(sp):
            def tile_source(layer, q, kind, group, part):
                if kind == "head":
                    cols = (HG_COLS if layer is HG else AT_COLS)[part]
                    return w_in[layer][:, :, ds(head(q, group) * P + cols, P)], KT
                if kind == "value":
                    col = (HG_VALUE if layer is HG else AT_VALUE)[group]
                    return w_in[layer][:, 2 * part:2 * part + 2, ds(q * (HQ * P) + col, HQ * P)], 2
                return w_out[layer][:, ds(q * HQ, HQ), part * 2 * P:(part + 1) * 2 * P], HQ

            def load(slot, source, k):
                sp.dma_start(raw[:, slot, :].rearrange("p (k n) -> p k n", k=k), source).then_inc(loaded[slot], 16)

            def load_after(layer, q, n, last):
                number, slot, _ = layer.tile(q, n)
                ahead = n + SLOTS
                if q is None:
                    where = (None, "value", ahead // 4, ahead % 4) if ahead < layer.pro else \
                        (0, *layer.kind(ahead - layer.pro, False))
                elif ahead < layer.quad_tiles(last):
                    what = layer.kind(ahead, last)
                    where = (q + 1 if what[0] == "value" else q, *what)
                elif not last:
                    where = (q + 1, *layer.kind(ahead - layer.T, False))
                elif layer is HG:
                    where, layer = (None, "value", 0, ahead - layer.quad_tiles(last)), AT
                else:
                    return
                wait_turn(sp, sp_met, w_ready, number + 1)
                load(slot, *tile_source(layer, 0 if where[0] is None else where[0], *where[1:]))

            for t in range(2):
                sp.dma_start(x_sb[:, 2 * t:2 * t + 2, :].rearrange("p a b -> p (a b)"), x_v[t]).then_inc(x_loaded[t], 16)
            sp.dma_start(ident[:, :], consts[:, 0:P]).then_inc(const_loaded[0], 16)
            sp.dma_start(prow[0:48, 0:P], hg_lb.rearrange("r (h p) -> (r h) p", p=P)).then_inc(const_loaded[1], 16)
            sp.dma_start(prow[48:64, 0:P], hg_norm.rearrange("r (h p) -> (r h) p", p=P)).then_inc(const_loaded[2], 16)
            sp.dma_start(prow[64:80, 0:P], ln_g.rearrange("r (h p) -> (r h) p", p=P)).then_inc(const_loaded[3], 16)
            for n in range(SLOTS):
                load(n, *tile_source(HG, 0, "value", 0, n))
            sp.dma_start(causal[:, :], consts[:, P:2 * P]).then_inc(const_loaded[4], 16)
            sp.dma_start(restart[:, :], consts[:, 2 * P:2 * P + S]).then_inc(const_loaded[4], 16)
            sp.dma_start(onehot_sb, onehot).then_inc(const_loaded[5], 16)
            sp.dma_start(relmask_sb, relmask).then_inc(const_loaded[6], 16)
            sp.dma_start(relb_sb, rel_bias).then_inc(const_loaded[7], 16)
            for t in range(2, ST):
                sp.wait_ge(x_T, KT * (t - 1))
                sp.dma_start(x_sb[:, 2 * (t % 2):2 * (t % 2) + 2, :].rearrange("p a b -> p (a b)"), x_v[t])\
                    .then_inc(x_loaded[t % 2], 16)
            sp.wait_ge(ext_ready, GROUPS)
            sp.dma_start(ext_dram.rearrange("g h e -> h g e"), ext_sb.rearrange("h (g e) -> h g e", g=GROUPS))\
                .then_inc(ext_stored, 16)
            for layer in (HG, AT):
                for n in range(layer.pro):
                    load_after(layer, None, n, False)

                def body(q, last):
                    for n in range(layer.quad_tiles(last)):
                        load_after(layer, q, n, last)
                quads(sp, body)
            sp.wait_ge(O_done, 2 * H)
            sp.dma_start(fg_bc, final_g.rearrange("(a d) -> a d", a=1).broadcast_to([P, D])).then_inc(const_loaded[0], 16)
            for t in range(ST):
                sp.wait_ge(fin_ready, t + 1)
                sp.dma_start(out_v[t], fin[:, D * (t % 2):D * (t % 2) + D]).then_inc(out_stored[t % 2], 16)
            for s in out_stored:
                sp.wait_ge(s, 16 * (ST // 2))
            sp.wait_ge(ext_stored, 16)

        @block.gpsimd
        def _(pool):
            nc.gpsimd.memset(ones[:, :], 1.0).then_inc(ones_ready, 1)
            natural = [d.rearrange("k (b p) -> p (k b)", p=P) for d in (nat_dram, res_dram)]
            residue = [d.rearrange("k (i r) -> i k r", r=RES) for d in (nat_dram, res_dram)]

            def load_bias(g):
                pool.dma_start(bias_n[:, :], bias_dram[ds(g, 1), :, 0:2 * P].rearrange("a p n -> p (a n)"))\
                    .then_inc(bias_loaded[0], 16)
                pool.dma_start(bias_r[:, :, :], bias_dram[ds(g, 1), :, 2 * P:].rearrange("a p (k n) -> p (a k) n", k=2))\
                    .then_inc(bias_loaded[1], 16)

            def exchange(g):
                wait_turn(pool, pool_met, nat_probs, 4 * g + 4)
                wait_turn(pool, pool_met, res_probs, 4 * g + 4)
                pool.dma_start(natural[0], stat[:, 0, :, :].rearrange("p k b -> p (k b)"), allow_slow_non_contiguous=True).then_inc(stat_a, 16)
                pool.dma_start(residue[1], stat[:, 1, :, :]).then_inc(stat_b, 16)
                wait_turn(pool, pool_met, stat_a, 32 * g + 16)
                pool.dma_start(stat_o[:, 1, :, :], residue[0]).then_inc(stat_a, 16)
                wait_turn(pool, pool_met, stat_b, 32 * g + 16)
                pool.dma_start(stat_o[:, 0, :, :].rearrange("p k b -> p (k b)"), natural[1], allow_slow_non_contiguous=True).then_inc(stat_b, 16)
                wait_turn(pool, pool_met, stat_a, 32 * g + 32)
                wait_turn(pool, pool_met, stat_b, 32 * g + 32)

            pool.wait_ge(ext_stored, 16)
            for g, first, n in ((0, P - 1, 2 * P), (1, 2 * P - 1, P), (2, 2 * P - 1, P)):
                to = (0, 2 * P, 3 * P)[g]
                pool.dma_start(bias_dram[:, :, to:to + n],
                               bass.AP(ext_dram.tensor, g * H * EXT + first, [[EXT, H], [-1, P], [1, n]]))\
                    .then_inc(bias_stored, 16)
            pool.wait_ge(bias_stored, 16 * GROUPS)
            load_bias(0)

            def body(q, last):
                for h in range(HQ):
                    g = head(q, h)
                    if not (last and h == HQ - 1):
                        wait_turn(pool, pool_met, bias_used, 2 * g + 2)
                        load_bias(g + 1)
                    exchange(g)
            quads(pool, body)

        @block.tensor
        def _(pe):
            def split_matmuls(bank, stationary, moving, first, last):
                ins = None
                for n, (a, b) in enumerate((("hi", "hi"), ("hi", "lo"), ("lo", "hi"))):
                    ins = nc.tensor.matmul(bank[:, :], stationary(a), moving(b),
                                           start=(first and n == 0), stop=(last and n == 2))
                return ins

            def open_bank(layer, q, e):
                _, bank, before = layer.event(q, e)
                if not (layer is HG and q is None and e < BANKS):
                    pe.wait_ge(bank_free[bank], before)
                return proj[bank]

            def head_tile(layer, q, n, half):
                number, slot, _ = layer.tile(q, n)
                event, bank, before = layer.event(q, n)
                if half == 0:
                    pe.wait_ge(w_ready, number + 1)
                    pe.wait_ge(bank_free[bank], before)
                for k in range(half * KT // 2, (half + 1) * KT // 2):
                    ins = split_matmuls(proj[bank], lambda a: w[a][:, slot, k * P:(k + 1) * P],
                                        lambda b: u[b][:, k, :], k == 0, k == KT - 1)
                if half:
                    ins.then_inc(proj_done, 1)

            def values(layer, q, group, s, half, wait_u=0):
                first = 4 * group + (0 if q is None else layer.heads)
                event, bank, before = layer.event(q, first + s)
                if half == 0 and not (layer is HG and q is None and s < BANKS):
                    pe.wait_ge(bank_free[bank], before)
                for i in range(2 * half, 2 * half + 2):
                    number, slot, _ = layer.tile(q, first + i)
                    if s == 0:
                        pe.wait_ge(w_ready, number + 1)
                    for k in (2 * i, 2 * i + 1):
                        if wait_u and s == 0:
                            pe.wait_ge(u_ready, wait_u + k)
                        cols = slice(s, S, RES) if group else slice(s * P, (s + 1) * P)
                        ins = split_matmuls(proj[bank], lambda a: u[a][:, k, cols],
                                            lambda b: w[b][:, slot, (k % 2) * S:(k % 2 + 1) * S], k == 0, k == KT - 1)
                    if i == 3:
                        ins.then_inc(proj_done, 1)
                    elif s == ST - 1:
                        ins.then_inc(value_tile_done, 1)

            def out_projection(layer, q, first):
                for i in range(4):
                    number, slot, _ = layer.tile(q, first + i)
                    pe.wait_ge(w_ready, number + 1)
                    for c in range(2):
                        event, bank, before = layer.event(q, first + 2 * i + c)
                        pe.wait_ge(bank_free[bank], before)
                        for k in range(HQ):
                            if i == 0 and c == 0:
                                pe.wait_ge(y_ready, (0 if layer is HG else H) + head(q, k) + 1)
                            ins = split_matmuls(proj[bank], lambda a: w[a][:, slot, (2 * k + c) * P:(2 * k + c + 1) * P],
                                                lambda b: y[b][:, k, :], k == 0, k == HQ - 1)
                        ins.then_inc(proj_done, 1)

            def sum_squares(first):
                for k in range(KT):
                    pe.wait_ge(sq_ready, first + k + 1)
                    nc.tensor.matmul(p_ss[:, :], ones[:, :], tmp[:, k % 2, :],
                                     start=(k == 0), stop=(k == KT - 1)).then_inc(ss_done, 1)

            pe.wait_ge(ones_ready, 1)
            pe.wait_ge(const_loaded[0], 16)
            for t in range(ST):
                pe.wait_ge(x_loaded[t % 2], 16 * (t // 2 + 1))
                for k in range(KT):
                    i = t * KT + k
                    if i >= 4 and i % 4 == 0:
                        pe.wait_ge(x_copied, i // 4 - (0 if i < 8 else 1))
                    nc.tensor.transpose(inner[(i // 4) % 2][:, (i % 4) * P:(i % 4 + 1) * P],
                                        x_sb[:, 2 * (t % 2) + k // 4, (k % 4) * P:(k % 4 + 1) * P],
                                        ident[:, :]).then_inc(x_T, 1)
                if t == 0:
                    for i in (1, 2, 3):
                        pe.wait_ge(const_loaded[i], 16)
                    nc.tensor.transpose(inner[2][:, 0:80], prow[0:80, 0:P], ident[0:80, 0:80]).then_inc(param_T, 1)
                    pe.wait_ge(param_ready, 1)
                    pe.wait_ge(const_loaded[5], 16)
                    pe.wait_ge(const_loaded[7], 16)
                    for g in range(GROUPS):
                        if g:
                            pe.wait_ge(ext_ready, g)
                        nc.tensor.matmul(inner[2][0:H, 0:EXT], relb_sb[:, g * H:(g + 1) * H],
                                         onehot_sb[:, g * EXT:(g + 1) * EXT], start=True, stop=True)\
                            .then_inc(ext_done, 1)
            sum_squares(0)

            for s in range(ST):
                for half in range(2):
                    values(HG, None, 0, s, half, wait_u=1)
            wait_emptied(pe, HG, None, HG.pro - 1)

            def scores(g):
                pe.wait_ge(q_ready, g + 1)
                pe.wait_ge(keys_ready, g + 1)
                for b in range(ST):
                    for j in range(NC):
                        ins = nc.tensor.matmul(p_sc[:, b * P + j * CH:b * P + (j + 1) * CH], keys[:, b, j, :],
                                               qd[:, b * P + j * CH:b * P + (j + 1) * CH], start=True, stop=True)
                ins.then_inc(scores_done, 1)
                for b in range(ST - 1):
                    ins = nc.tensor.transpose(p_kT[:, b * P:(b + 1) * P], keys[:, b, NC, :], ident[:, :])
                ins.then_inc(kT_done, 1)

            def updates(g, h):
                pe.wait_ge(kT_ready, g + 1)
                for b in range(ST - 1):
                    ins = nc.tensor.matmul(p_U[:, b * P:(b + 1) * P], kT[:, b, :], v_sb[0][:, b, h * P:(h + 1) * P],
                                           start=True, stop=True)
                ins.then_inc(U_done, 1)

            def outputs(g, h):
                pe.wait_ge(sT_ready, g + 1)
                pe.wait_ge(state_ready, g + 1)
                for b in range(ST):
                    s = slice(b * P, (b + 1) * P)
                    ins = nc.tensor.matmul(p_O[:, s], v_sb[0][:, b, h * P:(h + 1) * P], sT[:, s],
                                           start=True, stop=(b == 0))
                    if b:
                        ins = nc.tensor.matmul(p_O[:, s], state[:, b - 1, :], qs[:, s], start=False, stop=True)
                ins.then_inc(O_done, 1)

            def norm_sum(g):
                pe.wait_ge(osq_ready, g + 1)
                nc.tensor.matmul(p_ss[:, :], ones[:, :], enb[:, :], start=True, stop=True).then_inc(osum_done, 1)

            def recurrence(g, h, half):
                if half == 0:
                    scores(g)
                elif half == 1:
                    updates(g, h)
                elif half == 2:
                    outputs(g, h)
                elif half == 3:
                    norm_sum(g)

            def hg_body(q, last):
                for h in range(HQ):
                    for half in range(2 * HG.per_head):
                        head_tile(HG, q, HG.per_head * h + half // 2, half % 2)
                        if h:
                            recurrence(head(q, h - 1), h - 1, half)
                for half in range(2 * HG.pro):
                    if not last:
                        values(HG, q, 0, half // 2, half % 2)
                    recurrence(head(q, HQ - 1), HQ - 1, half)
                out_projection(HG, q, HG.heads + (0 if last else HG.pro))
                if not last:
                    wait_emptied(pe, HG, q, HG.heads + HG.pro - 1)
            quads(pe, hg_body)

            sum_squares(KT)
            for g in range(GROUPS):
                for s in range(ST):
                    for half in range(2):
                        values(AT, None, g, s, half, wait_u=0 if g else KT + 1)
            wait_emptied(pe, AT, None, AT.pro - 1)

            def natural_logits(q, h):
                wait_emptied(pe, AT, q, 7 * h + K0)
                for b in range(ST):
                    lo = max(b - 1, 0) * P
                    n = (b + 1) * P - lo
                    bank = p_S[b // 2]
                    at = (b % 2) * 2 * P
                    ins = nc.tensor.matmul(bank[:, at:at + n], qk[:, 0, b * P:(b + 1) * P], qk[:, 1, lo:lo + n],
                                           start=True, stop=True)
                    if b % 2:
                        ins.then_inc(nat_done, 1)

            def residue_logits(g, q, h):
                wait_emptied(pe, AT, q, 7 * h + K2)
                pe.wait_ge(nat_logits, g + 1)
                for r in range(RES):
                    for i in range(2):
                        s = slice(r * P, (r + 1) * P)
                        ins = nc.tensor.matmul(p_S[r // 2][:, ((r % 2) * 2 + i) * P:((r % 2) * 2 + i + 1) * P],
                                               qk[:, 2 + 2 * i, s], qk[:, 3 + 2 * i, s], start=True, stop=True)
                    if r % 2:
                        ins.then_inc(res_done, 1)

            def transposes(g, batches):
                for n in batches:
                    if n == 0:
                        pe.wait_ge(scaled, g + 1)
                    if n == 2:
                        pe.wait_ge(T_even, 2 * g + 1)
                    if n == 3:
                        pe.wait_ge(T_odd, 2 * g + 1)
                    for i in BATCHES[n]:
                        b, c = TILES[i]
                        if i < NATURAL:
                            src = probs[:, b, (c - b + 1 if b else 0) * P:(c - b + 2 if b else 1) * P]
                        else:
                            src = probs[:, ST + b, (c - 1) * P:c * P]
                        ins = nc.tensor.transpose(p_T[n % 2][:, (i % 4) * P:(i % 4 + 1) * P], src, ident[:, :])
                    ins.then_inc(T_done, 1)

            def attend(g, h):
                pe.wait_ge(T_even, 2 * g + 2)
                pe.wait_ge(T_odd, 2 * g + 2)
                for i, (b, c) in enumerate(TILES):
                    if i < NATURAL:
                        vals, o = v_sb[0][:, c, h * P:(h + 1) * P], p_O[:, b * P:(b + 1) * P]
                    else:
                        vals, o = v_sb[c][:, b, h * P:(h + 1) * P], p_O[:, b::RES]
                    ins = nc.tensor.matmul(o, vals, pT[:, i, :], start=(i == 0), stop=(i == len(TILES) - 1),
                                           skip_group_check=True)
                ins.then_inc(O_done, 1)

            def attention(g, h, half):
                if half == 3:
                    transposes(g, (0, 1))
                elif half == 4:
                    transposes(g, (2, 3))
                elif half == 5:
                    attend(g, h)

            def at_body(q, last):
                for h in range(HQ):
                    for half in range(2 * AT.per_head):
                        head_tile(AT, q, AT.per_head * h + half // 2, half % 2)
                        if h:
                            attention(head(q, h - 1), h - 1, half)
                        if half == 2 * K1:
                            natural_logits(q, h)
                        elif half == 2 * GA:
                            residue_logits(head(q, h), q, h)
                for half in range(2 * AT.pro):
                    if not last:
                        values(AT, q, half // 8, half // 2 % 4, half % 2)
                    attention(head(q, HQ - 1), HQ - 1, half)
                out_projection(AT, q, AT.heads + (0 if last else AT.pro))
                if not last:
                    wait_emptied(pe, AT, q, AT.heads + AT.pro - 1)
            quads(pe, at_body)

            wait_emptied(pe, AT, NQ - 1, AT.heads + KT - 1)
            for t in range(ST):
                for k in range(KT):
                    i = t * KT + k
                    if i >= 8 and i % 4 == 0:
                        pe.wait_ge(fin_copied, i // 4 - 1)
                    nc.tensor.transpose(inner[(i // 4) % 2][:, (i % 4) * P:(i % 4 + 1) * P],
                                        hT[:, k, t * P:(t + 1) * P], ident[:, :]).then_inc(fin_T, 1)

        @block.scalar
        def _(act):
            def split_hi(layer, q, n, last):
                number, slot, use = layer.tile(q, n)
                if layer is AT and last and n + SLOTS >= layer.quad_tiles(True):
                    return
                act.wait_ge(loaded[slot], use * 16 + 32)
                wait_tile_done(act, layer, q, n, last)
                nc.scalar.activation(w["hi"][:, slot, :], raw[:, slot, :], ACT.Copy).then_inc(hi_ready, 1)

            def copy_values(layer, q, group, e):
                _, bank, _ = layer.event(q, e)
                number = layer.event(q, e)[0]
                act.wait_ge(proj_done, number + 1)
                nc.scalar.activation(v_sb[group][:, (e - (0 if q is None else layer.heads)) % ST, :], proj[bank][:, :],
                                     ACT.Copy).then_inc(bank_free[bank], 1)

            def norm(which):
                for k in range(KT):
                    if which:
                        wait_emptied(act, HG, NQ - 1, HG.heads + k)
                    else:
                        act.wait_ge(x_copied, 2 * ST)
                    if k >= 2:
                        act.wait_ge(ss_done, which * KT + k - 1)
                    nc.scalar.activation(tmp[:, k % 2, :], hT[:, k, :], ACT.Square).then_inc(sq_ready, 1)
                act.wait_ge(ss_done, which * KT + KT)
                nc.scalar.activation(rstd[:, :], p_ss[:, :], ACT.Ln, scale=1.0 / D, bias=eps[:, :]).then_inc(rstd_step, 1)
                act.wait_ge(rstd_step, which + 1)
                nc.scalar.activation(rstd[:, :], rstd[:, :], ACT.Exp, scale=-0.5).then_inc(rstd_ready, 1)
                for k in range(KT):
                    act.wait_ge(u_made, which * KT + k + 1)
                    nc.scalar.activation(u["hi"][:, k, :], tmp[:, k % 2, :], ACT.Copy).then_inc(u_hi_ready, 1)

            nc.scalar.preload_act_table_set("natural_log_exp_and_others")
            act.wait_ge(eps_ready, 1)
            for n in range(SLOTS):
                act.wait_ge(loaded[n], 16)
                nc.scalar.activation(w["hi"][:, n, :], raw[:, n, :], ACT.Copy).then_inc(hi_ready, 1)
            act.wait_ge(lb_step, 3)
            nc.scalar.activation(param[:, 0:3 * H], param[:, 0:3 * H], ACT.Exp).then_inc(lb_exp, 1)
            norm(0)
            def value_events(layer, q, group, first):
                base = 4 * group + (0 if q is None else layer.heads)
                for s in range(first, ST):
                    if s == ST - 1:
                        for i in range(3):
                            split_hi(layer, q, base + i, False)
                    copy_values(layer, q, group, base + s)
                split_hi(layer, q, base + 3, False)

            value_events(HG, None, 0, 0)

            def kT_copy(g):
                act.wait_ge(kT_done, g + 1)
                nc.scalar.activation(kT[:, :, :].rearrange("p a b -> p (a b)"), p_kT[:, 0:(ST - 1) * P], ACT.Copy)\
                    .then_inc(kT_ready, 1)

            def square(g):
                act.wait_ge(O_done, g + 1)
                nc.scalar.activation(enb[:, :], p_O[:, :], ACT.Square).then_inc(osq_ready, 1)

            def out_rstd(g):
                act.wait_ge(osum_done, g + 1)
                nc.scalar.activation(rstd[:, :], p_ss[:, :], ACT.Ln, scale=1.0 / P, bias=eps[:, :]).then_inc(orstd_step, 1)
                act.wait_ge(orstd_step, g + 1)
                nc.scalar.activation(rstd[:, :], rstd[:, :], ACT.Exp, scale=-0.5).then_inc(orstd_ready, 1)

            def y_high(g, slot):
                act.wait_ge(y_made, g + 1)
                nc.scalar.activation(y["hi"][:, slot, :], y_f[:, :], ACT.Copy).then_inc(y_hi_ready, 1)

            def hg_body(q, last):
                for h in range(HQ):
                    g, before = head(q, h), head(q, h - 1) if h else None
                    number, bank, _ = HG.event(q, 3 * h + F_)
                    if h:
                        kT_copy(before)
                    act.wait_ge(proj_done, number + 1)
                    nc.scalar.activation(ef[:, :], proj[bank][:, :], ACT.Exp, scale=-1.0).then_inc(bank_free[bank], 1)
                    split_hi(HG, q, 3 * h + F_, last)
                    act.wait_ge(f_ready, g + 1)
                    nc.scalar.activation(lnf[:, :], fg[:, :], ACT.Ln).then_inc(lnf_ready, 1)
                    if h:
                        square(before)
                    act.wait_ge(b_ready, g + 1)
                    nc.scalar.activation(eb[:, :], bb[:, :], ACT.Exp).then_inc(eb_ready, 1)
                    if h:
                        out_rstd(before)
                    nc.scalar.activation(enb[:, :], bb[:, :], ACT.Exp, scale=-1.0).then_inc(eb_ready, 1)
                    split_hi(HG, q, 3 * h + Q_, last)
                    if h:
                        y_high(before, h - 1)
                    number, bank, _ = HG.event(q, 3 * h + G_)
                    act.wait_ge(proj_done, number + 1)
                    nc.scalar.activation(eg[:, :], proj[bank][:, :], ACT.Exp, scale=-1.0).then_inc(expg_ready, 1)
                    split_hi(HG, q, 3 * h + G_, last)
                g = head(q, HQ - 1)
                kT_copy(g)
                square(g)
                if not last:
                    copy_values(HG, q, 0, HG.heads)
                    copy_values(HG, q, 0, HG.heads + 1)
                out_rstd(g)
                y_high(g, HQ - 1)
                if not last:
                    value_events(HG, q, 0, 2)
                for n in range(HG.quad_tiles(last) - 4, HG.quad_tiles(last)):
                    split_hi(HG, q, n, last)
            quads(act, hg_body)

            norm(1)
            for g in range(GROUPS):
                value_events(AT, None, g, 0)

            def exps(g, first, logits, signal):
                act.wait_ge(logits, g + 1)
                for b in range(ST):
                    i = first + b
                    n = P if i == 0 else 2 * P
                    nc.scalar.activation(probs[:, i, 0:n], probs[:, i, 0:n], ACT.Exp, bias=negm[:, i:i + 1],
                                         accum_out=stat[:, i // ST, 1, b:b + 1]).then_inc(signal, 1)

            def merge_exps(g):
                act.wait_ge(merge_in, g + 1)
                nc.scalar.activation(merge[:, :, :, :], both[:, :, :, :], ACT.Exp).then_inc(merge_exp, 1)

            def copy_odd(g):
                for n, b in enumerate((1, 3)):
                    act.wait_ge(T_done, 4 * g + b + 1)
                    nc.scalar.activation(pT[:, BATCHES[b][0]:BATCHES[b][-1] + 1, :],
                                         p_T[1][:, 0:len(BATCHES[b]) * P].rearrange("p (a b) -> p a b", b=P),
                                         ACT.Copy).then_inc(T_odd, 1)

            def at_body(q, last):
                for h in range(HQ):
                    g, before = head(q, h), head(q, h - 1) if h else None
                    for i in range(7):
                        number, bank, _ = AT.event(q, 7 * h + i)
                        if i == Q1 and h:
                            merge_exps(before)
                            copy_odd(before)
                        act.wait_ge(proj_done, number + 1)
                        if i == GA:
                            nc.scalar.activation(eg[:, :], proj[bank][:, :], ACT.Exp, scale=-1.0).then_inc(expg_ready, 1)
                        else:
                            o, src = qk[:, i, :], proj[bank][:, :]
                            if i >= Q1:
                                o = qk[:, i, :].rearrange("p (r i) -> p r i", r=RES)
                                src = proj[bank][:, :].rearrange("p (i r) -> p r i", r=RES)
                            nc.scalar.activation(o, src, ACT.Copy, scale=QSCALE if i in (Q0, Q1, Q2) else 1.0)\
                                .then_inc(bank_free[bank], 1)
                        split_hi(AT, q, 7 * h + i, last)
                        if i == Q1 and h:
                            y_high(before + H, h - 1)
                        if i == K2:
                            exps(g, 0, nat_logits, nat_probs)
                    exps(g, ST, res_logits, res_probs)
                g = head(q, HQ - 1)
                merge_exps(g)
                copy_odd(g)
                if not last:
                    act.wait_ge(O_done, H + g + 1)
                    copy_values(AT, q, 0, AT.heads)
                y_high(g + H, HQ - 1)
                if not last:
                    for group in range(GROUPS):
                        value_events(AT, q, group, 0 if group else 1)
                for n in range(AT.quad_tiles(last) - 4, AT.quad_tiles(last)):
                    split_hi(AT, q, n, last)
            quads(act, at_body)

            for t in range(ST):
                act.wait_ge(fin_copied, 2 * t + 2)
                nc.scalar.activation(raw[:, 0, :], fin[:, D * (t % 2):D * (t % 2) + D], ACT.Square,
                                     accum_out=cols[:, t:t + 1]).then_inc(fin_sq, 1)
                act.wait_ge(fin_sq, t + 1)
                nc.scalar.activation(cols[:, 4 + t:5 + t], cols[:, t:t + 1], ACT.Ln, scale=1.0 / D, bias=eps[:, :])\
                    .then_inc(fin_step, 1)
                act.wait_ge(fin_step, t + 1)
                nc.scalar.activation(cols[:, 8 + t:9 + t], cols[:, 4 + t:5 + t], ACT.Exp, scale=-0.5).then_inc(fin_rstd, 1)

        @block.vector
        def _(dve):
            def split_lo(layer, q, n, last):
                if layer is AT and last and n + SLOTS >= layer.quad_tiles(True):
                    return
                number, slot, _ = layer.tile(q, n)
                dve.wait_ge(hi_ready, number + SLOTS + 1)
                nc.vector.tensor_tensor(w["lo"][:, slot, :], raw[:, slot, :], w["hi"][:, slot, :].bitcast(F32),
                                        ALU.subtract).then_inc(w_ready, 1)

            def norm(which):
                dve.wait_ge(rstd_ready, which + 1)
                for k in range(KT + 1):
                    if k < KT:
                        if k >= 2:
                            dve.wait_ge(u_ready, which * KT + k - 1)
                        nc.vector.scalar_tensor_tensor(out=tmp[:, k % 2, :], in0=hT[:, k, :],
                                                       scalar=param[:, 64 + which * KT + k:65 + which * KT + k],
                                                       in1=rstd[:, :], op0=ALU.mult, op1=ALU.mult).then_inc(u_made, 1)
                    if k:
                        dve.wait_ge(u_hi_ready, which * KT + k)
                        nc.vector.tensor_tensor(u["lo"][:, k - 1, :], tmp[:, (k - 1) % 2, :],
                                                u["hi"][:, k - 1, :].bitcast(F32), ALU.subtract).then_inc(u_ready, 1)

            nc.vector.memset(eps[:, :], EPS).then_inc(eps_ready, 1)
            for i in range(2 * ST):
                t, half = i // 2, i % 2
                dve.wait_ge(x_T, 4 * i + 4)
                nc.vector.tensor_copy(hT[:, 4 * half:4 * half + 4, t * P:(t + 1) * P],
                                      inner[i % 2][:, :].rearrange("p (a b) -> p a b", b=P)).then_inc(x_copied, 1)
                if i == 1:
                    dve.wait_ge(param_T, 1)
                    nc.vector.tensor_copy(param[:, :], inner[2][:, 0:80]).then_inc(param_ready, 1)
                    dve.wait_ge(param_ready, 1)
                    nc.vector.tensor_tensor(lb[:, :], param[:, 0:H], param[:, H:2 * H], ALU.max).then_inc(lb_step, 1)
                    dve.wait_ge(lb_step, 1)
                    nc.vector.tensor_tensor(oml[:, :], lb[:, :], param[:, 2 * H:3 * H], ALU.max).then_inc(lb_step, 1)
                    dve.wait_ge(lb_step, 2)
                    for r in range(3):
                        ins = nc.vector.tensor_tensor(param[:, r * H:(r + 1) * H], param[:, r * H:(r + 1) * H],
                                                      oml[:, :], ALU.subtract)
                    ins.then_inc(lb_step, 1)
                    dve.wait_ge(const_loaded[6], 16)
                    for g in range(GROUPS):
                        dve.wait_ge(ext_done, g + 1)
                        nc.vector.tensor_tensor(ext_sb[:, g * EXT:(g + 1) * EXT], inner[2][0:H, 0:EXT],
                                                relmask_sb[:, g * EXT:(g + 1) * EXT], ALU.add).then_inc(ext_ready, 1)
            for n in range(SLOTS):
                dve.wait_ge(hi_ready, n + 1)
                nc.vector.tensor_tensor(w["lo"][:, n, :], raw[:, n, :], w["hi"][:, n, :].bitcast(F32),
                                        ALU.subtract).then_inc(w_ready, 1)
            dve.wait_ge(lb_exp, 1)
            steps = 3

            def step(ins):
                nonlocal steps
                steps += 1
                ins.then_inc(lb_step, 1)
                dve.wait_ge(lb_step, steps)

            step(nc.vector.tensor_tensor(lb[:, :], param[:, 0:H], param[:, H:2 * H], ALU.add))
            step(nc.vector.tensor_tensor(oml[:, :], lb[:, :], param[:, 2 * H:3 * H], ALU.add))
            step(nc.vector.reciprocal(oml[:, :], oml[:, :]))
            step(nc.vector.tensor_tensor(lb[:, :], param[:, 0:H], oml[:, :], ALU.mult))
            step(nc.vector.tensor_scalar(oml[:, :], lb[:, :], -1.0, 1.0, ALU.mult, ALU.add))
            norm(0)
            dve.wait_ge(ext_stored, 16)
            step(nc.vector.memset(keys[:, :, :, :], 0.0))
            step(nc.vector.memset(dec[:, :, :], 1.0))
            dve.wait_ge(const_loaded[4], 32)
            for n in range(HG.pro):
                split_lo(HG, None, n, False)

            def gate(link, layer, q, h, g, event):
                _, bank, _ = layer.event(q, event)
                dve.wait_ge(expg_ready, g + 1)
                link(nc.vector.tensor_scalar(eg[:, :], eg[:, :], 1.0, None, ALU.add))
                link(nc.vector.reciprocal(eg[:, :], eg[:, :]))
                nc.vector.tensor_tensor(sg[:, :], proj[bank][:, :], eg[:, :], ALU.mult).then_inc(bank_free[bank], 1)

            def mask_scores(g):
                dve.wait_ge(scores_done, g + 1)
                nc.vector.tensor_tensor(sT[:, :].rearrange("p (b c) -> p b c", b=ST),
                                        p_sc[:, :].rearrange("p (b c) -> p b c", b=ST),
                                        causal[:, :].unsqueeze(1).broadcast_to([P, ST, P]), ALU.mult)\
                    .then_inc(sT_ready, 1)

            def states(link, g):
                dve.wait_ge(U_done, g + 1)
                link(nc.vector.tensor_copy(state[:, 0, :], p_U[:, 0:P]))
                link(nc.vector.scalar_tensor_tensor(out=state[:, 1, :], in0=state[:, 0, :], scalar=dec[:, 1, NC:NC + 1],
                                                    in1=p_U[:, P:2 * P], op0=ALU.mult, op1=ALU.add))
                nc.vector.scalar_tensor_tensor(out=state[:, 2, :], in0=state[:, 1, :], scalar=dec[:, 2, NC:NC + 1],
                                               in1=p_U[:, 2 * P:3 * P], op0=ALU.mult, op1=ALU.add)\
                    .then_inc(state_ready, 1)

            def forget(link, q, h, g):
                wait_emptied(dve, HG, q, 3 * h + F_)
                link(nc.vector.tensor_scalar(ef[:, :], ef[:, :], 1.0, None, ALU.add))
                link(nc.vector.reciprocal(ef[:, :], ef[:, :]))
                nc.vector.tensor_scalar(fg[:, :], ef[:, :], oml[:, ds(g, 1)], lb[:, ds(g, 1)], ALU.mult, ALU.add)\
                    .then_inc(f_ready, 1)
                dve.wait_ge(f_ready, g + 1)
                nc.vector.tensor_scalar(kk[:, :], fg[:, :], -1.0, 1.0, ALU.mult, ALU.add)

            def cumulate(g):
                dve.wait_ge(lnf_ready, g + 1)
                nc.vector.tensor_tensor_scan(bb[:, :], restart[:, :], lnf[:, :], 0.0, ALU.mult, ALU.add)\
                    .then_inc(b_ready, 1)

            def decays(link, q, h, g):
                number, bank, _ = HG.event(q, 3 * h + Q_)
                chunk = lambda t: t[:, :].rearrange("p (b j c) -> p b j c", b=ST, j=NC)
                A = chunk(eb)[:, :, :, CH - 1:CH]
                dve.wait_ge(proj_done, number + 1)
                dve.wait_ge(eb_ready, 2 * g + 2)
                nc.vector.tensor_tensor(qd[:, :], proj[bank][:, :], eb[:, :], ALU.mult).then_inc(bank_free[bank], 1)
                flat = keys[:, :, :, :].rearrange("p b s k -> p b (s k)")
                own = bass.AP(flat.tensor, flat.offset, [list(flat.ap[0]), [(NC + 1) * P, ST], [P + CH, NC], [1, CH]])
                after = bass.AP(flat.tensor, flat.offset + P, [list(flat.ap[0]), [(NC + 1) * P, ST], [P + CH, NC], [1, CH]])
                link(nc.vector.tensor_tensor(own, chunk(kk), chunk(enb), ALU.mult))
                link(nc.vector.tensor_tensor(after, own, A.broadcast_to([P, ST, NC, CH]), ALU.mult))
                link(nc.vector.tensor_copy(dec[:, :, 1:2], A[:, :, 0, :]))
                for j in range(1, NC):
                    link(nc.vector.tensor_tensor(dec[:, :, j + 1:j + 2], dec[:, :, j:j + 1], A[:, :, j, :], ALU.mult))
                    ins = nc.vector.tensor_tensor(keys[:, :, j + 1, 0:j * CH], keys[:, :, j, 0:j * CH],
                                                  A[:, :, j, :].broadcast_to([P, ST, j * CH]), ALU.mult)
                    if j < NC - 1:
                        link(ins)
                    else:
                        ins.then_inc(keys_ready, 1)
                nc.vector.tensor_tensor(chunk(qs), chunk(qd), dec[:, :, 0:NC].unsqueeze(3).broadcast_to([P, ST, NC, CH]),
                                        ALU.mult).then_inc(q_ready, 1)

            def hg_output(link, g, slot):
                dve.wait_ge(orstd_ready, g + 1)
                link(nc.vector.tensor_tensor(y_f[:, :], p_O[:, :], rstd[:, :], ALU.mult))
                nc.vector.scalar_tensor_tensor(out=y_f[:, :], in0=y_f[:, :], scalar=param[:, ds(g + 3 * H, 1)],
                                               in1=sg[:, :], op0=ALU.mult, op1=ALU.mult).then_inc(y_made, 1)

            def y_low(g, slot):
                dve.wait_ge(y_hi_ready, g + 1)
                nc.vector.tensor_tensor(y["lo"][:, slot, :], y_f[:, :], y["hi"][:, slot, :].bitcast(F32), ALU.subtract)\
                    .then_inc(y_ready, 1)

            def add_out(layer, q, n, e, last):
                for i in range(4):
                    for c in range(2):
                        k = 2 * i + c
                        number, bank, _ = layer.event(q, e + k)
                        dve.wait_ge(proj_done, number + 1)
                        nc.vector.tensor_tensor(hT[:, k, :], hT[:, k, :], proj[bank][:, :], ALU.add)\
                            .then_inc(bank_free[bank], 1)
                    split_lo(layer, q, n + i, last)

            def hg_body(q, last):
                links = 0

                def link(ins):
                    nonlocal links
                    links += 1
                    ins.then_inc(link_hg, 1)
                    dve.wait_ge(link_hg, q * LINKS_HG + links)

                for h in range(HQ):
                    g, before = head(q, h), head(q, h - 1) if h else None
                    if h:
                        gate(link, HG, q, h - 1, before, 3 * (h - 1) + G_)
                        mask_scores(before)
                        states(link, before)
                    forget(link, q, h, g)
                    split_lo(HG, q, 3 * h + F_, last)
                    cumulate(g)
                    if h:
                        hg_output(link, before, h - 1)
                    decays(link, q, h, g)
                    split_lo(HG, q, 3 * h + Q_, last)
                    if h:
                        y_low(before, h - 1)
                    split_lo(HG, q, 3 * h + G_, last)
                g = head(q, HQ - 1)
                gate(link, HG, q, HQ - 1, g, 3 * (HQ - 1) + G_)
                mask_scores(g)
                states(link, g)
                hg_output(link, g, HQ - 1)
                y_low(g, HQ - 1)
                if not last:
                    for n in range(4):
                        split_lo(HG, q, HG.heads + n, last)
                rest = HG.heads + (0 if last else HG.pro)
                add_out(HG, q, rest, rest, last)
                assert links == LINKS_HG, links
            quads(dve, hg_body)

            norm(1)
            for n in range(AT.pro):
                split_lo(AT, None, n, False)

            def biases(g, first, tile, done, loaded_, banks, signal, link):
                dve.wait_ge(loaded_, 16 * g + 16)
                for i in range(2):
                    dve.wait_ge(done, 2 * g + i + 1)
                    if first == 0 and i == 0:
                        nc.vector.tensor_tensor(probs[:, 0, 0:P], banks[0][:, 0:P], tile[:, P:2 * P], ALU.add)
                        ins = nc.vector.tensor_tensor(probs[:, 1, :], banks[0][:, 2 * P:4 * P], tile, ALU.add)
                    else:
                        ins = nc.vector.tensor_tensor(probs[:, first + 2 * i:first + 2 * i + 2, :],
                                                      banks[i][:, :].rearrange("p (a b) -> p a b", a=2),
                                                      tile.unsqueeze(1).broadcast_to([P, 2, 2 * P]), ALU.add)
                ins.then_inc(bias_used, 1)
                dve.wait_ge(bias_used, 2 * g + (2 if first else 1))
                if first == 0:
                    nc.vector.tensor_reduce(stat[:, 0, 0, 0:1], probs[:, 0, 0:P], AX.X, ALU.max)
                    link(nc.vector.tensor_reduce(stat[:, 0, 0, 1:ST], probs[:, 1:ST, :], AX.X, ALU.max))
                else:
                    link(nc.vector.tensor_reduce(stat[:, 1, 0, :], probs[:, ST:2 * ST, :], AX.X, ALU.max))
                nc.vector.tensor_scalar(negm[:, first:first + ST], stat[:, first // ST, 0, :], -1.0, None, ALU.mult)\
                    .then_inc(signal, 1)

            def merge_and_scale(link, g):
                dve.wait_ge(stat_a, 32 * g + 32)
                dve.wait_ge(stat_b, 32 * g + 32)
                link(nc.vector.tensor_tensor(share[:, :, :], stat[:, :, 0, :], stat_o[:, :, 0, :], ALU.max))
                nc.vector.tensor_tensor(both[:, 0, :, :], stat[:, :, 0, :], share[:, :, :], ALU.subtract)
                nc.vector.tensor_tensor(both[:, 1, :, :], stat_o[:, :, 0, :], share[:, :, :], ALU.subtract).then_inc(merge_in, 1)
                dve.wait_ge(merge_exp, g + 1)
                nc.vector.tensor_tensor(both[:, 0, :, :], merge[:, 0, :, :], stat[:, :, 1, :], ALU.mult)
                link(nc.vector.tensor_tensor(both[:, 1, :, :], merge[:, 1, :, :], stat_o[:, :, 1, :], ALU.mult))
                link(nc.vector.tensor_tensor(share[:, :, :], both[:, 0, :, :], both[:, 1, :, :], ALU.add))
                link(nc.vector.reciprocal(share[:, :, :], share[:, :, :]))
                link(nc.vector.tensor_tensor(share[:, :, :], share[:, :, :], merge[:, 0, :, :], ALU.mult))
                for i in range(2 * ST):
                    n = P if i == 0 else 2 * P
                    ins = nc.vector.tensor_scalar(probs[:, i, 0:n], probs[:, i, 0:n], share[:, i // ST, i % ST:i % ST + 1], None, ALU.mult)
                ins.then_inc(scaled, 1)

            def copy_even(g):
                for b in (0, 2):
                    dve.wait_ge(T_done, 4 * g + b + 1)
                    nc.vector.tensor_copy(pT[:, BATCHES[b][0]:BATCHES[b][-1] + 1, :],
                                          p_T[0][:, 0:len(BATCHES[b]) * P].rearrange("p (a b) -> p a b", b=P))\
                        .then_inc(T_even, 1)

            def at_output(g):
                dve.wait_ge(O_done, H + g + 1)
                nc.vector.tensor_tensor(y_f[:, :], p_O[:, :], sg[:, :], ALU.mult).then_inc(y_made, 1)

            def at_body(q, last):
                links = 0

                def link(ins):
                    nonlocal links
                    links += 1
                    ins.then_inc(link_at, 1)
                    dve.wait_ge(link_at, q * LINKS_AT + links)

                bias_r_flat = bias_r[:, :, :].rearrange("p a b -> p (a b)")
                for h in range(HQ):
                    g, before = head(q, h), head(q, h - 1) if h else None
                    for i in range(7):
                        split_lo(AT, q, 7 * h + i, last) if i not in (Q1,) else None
                        if i == K0 and h:
                            merge_and_scale(link, before)
                            copy_even(before)
                        if i == Q1:
                            split_lo(AT, q, 7 * h + i, last)
                            if h:
                                at_output(before)
                                y_low(before + H, h - 1)
                        if i == K1:
                            biases(g, 0, bias_n[:, :], nat_done, bias_loaded[0], p_S, nat_logits, link)
                        if i == GA:
                            biases(g, ST, bias_r_flat, res_done, bias_loaded[1], p_S, res_logits, link)
                            gate(link, AT, q, h, H + g, 7 * h + GA)
                g = head(q, HQ - 1)
                merge_and_scale(link, g)
                copy_even(g)
                at_output(g)
                y_low(g + H, HQ - 1)
                if not last:
                    for n in range(AT.pro):
                        split_lo(AT, q, AT.heads + n, last)
                rest = AT.heads + (0 if last else AT.pro)
                add_out(AT, q, rest, rest, last)
                assert links == LINKS_AT, links
            quads(dve, at_body)

            dve.wait_ge(const_loaded[0], 32)
            for t in range(ST):
                tile = fin[:, D * (t % 2):D * (t % 2) + D]
                if t >= 2:
                    dve.wait_ge(out_stored[t % 2], 16 * (t // 2))
                for i in range(2):
                    dve.wait_ge(fin_T, KT * t + 4 * i + 4)
                    nc.vector.tensor_copy(tile[:, i * S:(i + 1) * S], inner[(2 * t + i) % 2][:, :]).then_inc(fin_copied, 1)
                dve.wait_ge(fin_rstd, t + 1)
                nc.vector.scalar_tensor_tensor(out=tile, in0=tile, scalar=cols[:, 8 + t:9 + t], in1=fg_bc,
                                               op0=ALU.mult, op1=ALU.mult).then_inc(fin_ready, 1)


def bucket_of(dist):
    exact = BUCKETS // 2
    df = np.maximum(dist, 1).astype(np.float32)
    large = exact + (np.log(df / np.float32(exact)) / np.float32(np.log(2048 / exact)) * np.float32(BUCKETS - exact)).astype(np.int32)
    return np.where(dist < exact, dist, np.minimum(large, BUCKETS - 1))


def shape_constants():
    consts = np.zeros((P, 2 * P + S), np.float32)
    consts[:, 0:P] = np.eye(P)
    consts[:, P:2 * P] = np.triu(np.ones((P, P)))
    consts[:, 2 * P:] = (np.arange(S) % CH != 0)
    onehot = np.zeros((BUCKETS, GROUPS, EXT), np.float32)
    relmask = np.full((H, GROUPS, EXT), MASKED, np.float32)
    for g, (window, dilation) in enumerate(((128, 1), (512, 4), (2048, 16))):
        order = 1 if g == 0 else RES
        for e in range(EXT):
            apart = 2 * P - 1 - e
            dist = apart * order
            if apart >= 0 and dist % dilation == 0 and dist <= window:
                onehot[bucket_of(np.array(dist)), g, e] = 1.0
                relmask[:, g, e] = 0.0
    return consts, onehot.reshape(BUCKETS, -1), relmask.reshape(H, -1)


def kernel(**inputs):
    import concourse.bacc as bacc
    from concourse.bass_utils import run_bass_kernel_spmd

    nc = bacc.Bacc("TRN2", target_bir_lowering=False, num_devices=1)
    consts, onehot, relmask = shape_constants()
    a = {n: np.ascontiguousarray(v) for n, v in inputs.items()}
    arrays = {
        "x": a["x"].reshape(S, D), "ln_g": a["ln_g"], "hg_w_in": a["hg_w_in"].reshape(D, -1),
        "hg_lb": a["hg_lb_logits"], "hg_norm": a["hg_norm_g"], "hg_w_out": a["hg_w_out"].reshape(W, D),
        "at_w_in": a["att_w_in"].reshape(D, -1), "at_w_out": a["att_w_out"].reshape(W, D),
        "rel_bias": a["rel_bias"], "final_g": a["final_g"], "consts": consts, "onehot": onehot, "relmask": relmask,
    }
    args = [nc.dram_tensor(n, v.shape, F32, kind="ExternalInput").ap() for n, v in arrays.items()]
    out = nc.dram_tensor("out", (S, D), F32, kind="ExternalOutput").ap()
    program(nc, *args, out)
    result = run_bass_kernel_spmd(nc, [arrays], core_ids=[0])
    return result.results[0]["out"].reshape(1, S, D)
```

```python
from contextlib import ExitStack

import numpy as np

import concourse.bass as bass
from concourse import mybir

F32 = mybir.dt.float32
F32R = mybir.dt.float32r
ALU = mybir.AluOpType
ACT = mybir.ActivationFunctionType
AX = mybir.AxisListType
ds = bass.ds

P = 128
S = 512
D = 1024
W = 2048
KT = D // P
H = W // P
HQ = 4
NQ = H // HQ
ST = S // P
CH = 32
NC = P // CH
GROUPS = 3
RES = 4
BUCKETS = 32
EPS = 1e-6
QSCALE = float(P) ** -0.5
MASKED = -1e30
SLOTS = 4
TW = 1024
BANKS = 3
EXT = 384


class Layer:

    def __init__(self, tile0, event0, value0, per_head, groups):
        self.value0 = value0
        self.per_head, self.groups = per_head, groups
        self.tile0, self.event0 = tile0, event0
        self.pro = 4 * groups
        self.heads = HQ * per_head
        self.T = self.heads + self.pro + 4
        self.EV = self.heads + self.pro + 8
        assert self.T % SLOTS == 0 and self.EV % BANKS == 0 and tile0 % SLOTS == 0
        self.tiles = self.pro + (NQ - 1) * self.T + self.heads + 4
        self.events = self.pro + (NQ - 1) * self.EV + self.heads + 16

    def tile(self, q, n):
        first = self.tile0 + n + (0 if q is None else self.pro)
        off = 0 if q is None else q * self.T
        turn = 0 if q is None else q * (self.T // SLOTS)
        return off + first, first % SLOTS, turn + first // SLOTS

    def event(self, q, n):
        first = self.event0 + n + (0 if q is None else self.pro)
        off = 0 if q is None else q * self.EV
        turn = 0 if q is None else q * (self.EV // BANKS)
        return off + first, first % BANKS, turn + first // BANKS

    def kind(self, n, last):
        if n < self.heads:
            return "head", n // self.per_head, n % self.per_head
        n -= self.heads
        if not last:
            if n < self.pro:
                return "value", n // 4, n % 4
            n -= self.pro
        return "out", 0, n

    def quad_tiles(self, last):
        return self.heads + 4 + (0 if last else self.pro)


HG = Layer(0, 0, 0, 3, 1)
AT = Layer(HG.tiles, HG.events, 3 * NQ * HG.groups, 7, GROUPS)
HG_COLS = (1 * W, 0 * W, 3 * W)
AT_COLS = (0, W, 3 * W, 4 * W, 6 * W, 7 * W, 9 * W)
HG_VALUE = (2 * W,)
AT_VALUE = (2 * W, 5 * W, 8 * W)
F_, Q_, G_ = 0, 1, 2
Q0, K0, Q1, K1, Q2, K2, GA = range(7)
LINKS_HG = 4 * 11
LINKS_AT = 4 * 7
TILES = [(0, 0)] + [(b, c) for b in range(1, ST) for c in (b - 1, b)] + [(r, g) for r in range(RES) for g in (1, 2)]
NATURAL = 2 * ST - 1
BATCHES = [range(i, min(i + 4, len(TILES))) for i in range(0, len(TILES), 4)]


def program(nc, x, ln_g, hg_w_in, hg_lb, hg_norm, hg_w_out, at_w_in, at_w_out, rel_bias, final_g,
            consts, onehot, relmask, out):
    ctx = ExitStack()
    with ctx:
        def sb(name, shape, dt=F32):
            return ctx.enter_context(nc.sbuf_tensor(name, shape, dt))

        def sem(name):
            return ctx.enter_context(nc.semaphore(name))

        x_v = x.rearrange("(t p) d -> t p d", p=P)
        out_v = out.rearrange("(t p) d -> t p d", p=P)
        w_in = {HG: hg_w_in.rearrange("(k p) n -> p k n", p=P), AT: at_w_in.rearrange("(k p) n -> p k n", p=P)}
        w_out = {HG: hg_w_out.rearrange("(k p) n -> p k n", p=P), AT: at_w_out.rearrange("(k p) n -> p k n", p=P)}
        ext_dram = nc.dram_tensor("ext_rows", [GROUPS, H, EXT], F32, kind="Internal").ap()
        bias_dram = nc.dram_tensor("bias_tiles", [H, P, 4 * P], F32, kind="Internal").ap()
        nat_dram = nc.dram_tensor("natural_stats", [2, S], F32, kind="Internal").ap()
        res_dram = nc.dram_tensor("residue_stats", [2, S], F32, kind="Internal").ap()

        ident = sb("ident", [P, P])
        causal = sb("causal", [P, P])
        restart = sb("restart", [P, S])
        ones = sb("ones", [P, P])
        param = sb("param", [P, 80])
        lb = sb("lb", [P, H])
        oml = sb("oml", [P, H])
        eps = sb("eps", [P, 1])
        u = {"hi": sb("u_hi", [P, KT, S], F32R), "lo": sb("u_lo", [P, KT, S], F32R)}
        hT = sb("hT", [P, KT, S])
        raw = sb("raw", [P, SLOTS, TW])
        w = {"hi": sb("w_hi", [P, SLOTS, TW], F32R), "lo": sb("w_lo", [P, SLOTS, TW], F32R)}
        y = {"hi": sb("y_hi", [P, HQ, S], F32R), "lo": sb("y_lo", [P, HQ, S], F32R)}
        v_sb = [sb(f"v{g}", [P, ST, S]) for g in range(GROUPS)]
        y_f = sb("y_f", [P, S])
        eg = sb("eg", [P, S])
        sg = sb("sg", [P, S])
        tmp = sb("tmp", [P, 2, S])
        rstd = sb("rstd", [P, S])
        rows = sb("rows", [P, 10, S])
        ef, fg, kk, lnf, bb, eb, enb, qd, qs, sT = [rows[:, i, :] for i in range(10)]
        keys = sb("keys", [P, ST, NC + 1, P])
        dec = sb("dec", [P, ST, NC + 1])
        kT = sb("kT", [P, ST - 1, P])
        state = sb("state", [P, ST - 1, P])
        qk = sb("qk", [P, 6, S])
        flat_rows = rows[:, :, :].rearrange("p a b -> p (a b)")
        pT = flat_rows[:, 0:len(TILES) * P].rearrange("p (a b) -> p a b", b=P)
        probs = flat_rows[:, 4 * S:8 * S].rearrange("p (a b) -> p a b", b=2 * P)
        bias_n = sb("bias_n", [P, 2 * P])
        bias_r = sb("bias_r", [P, 2, P])
        stat = sb("stat", [P, 2, 2, ST])
        stat_o = sb("stat_o", [P, 2, 2, ST])
        negm = sb("negm", [P, 2 * ST])
        both = sb("both", [P, 2, 2, ST])
        merge = sb("merge", [P, 2, 2, ST])
        share = sb("share", [P, 2, ST])
        cols = sb("cols", [P, 16])
        x_sb = qk
        prow = probs[:, :, :].rearrange("p a b -> p (a b)")
        onehot_sb = pT[:, :, :].rearrange("p a b -> p (a b)")[0:BUCKETS, 0:GROUPS * EXT]
        relmask_sb = keys[:, :, :, :].rearrange("p a b c -> p (a b c)")[0:H, 0:GROUPS * EXT]
        ext_sb = keys[:, :, :, :].rearrange("p a b c -> p (a b c)")[0:H, GROUPS * EXT:2 * GROUPS * EXT]
        relb_sb = bias_n[0:BUCKETS, 0:GROUPS * H]
        fin = [v_sb[1 + t // 2][:, 2 * (t % 2):2 * (t % 2) + 2, :] for t in range(ST)]
        fg_bc = v_sb[0][:, 0:2, :].rearrange("p a b -> p (a b)")

        proj = [ctx.enter_context(nc.psum_tensor(f"proj{i}", [P, S], F32)) for i in range(BANKS)]
        inner = [ctx.enter_context(nc.psum_tensor(f"inner{i}", [P, S], F32)) for i in range(5)]
        p_sc, p_kT, p_U, p_O, p_ss = inner
        p_S = inner[0:2]
        p_T = (inner[2], inner[4])

        x_loaded = [sem(f"x_loaded{i}") for i in range(2)]
        const_loaded = [sem(f"const_loaded{i}") for i in range(8)]
        loaded = [sem(f"loaded{i}") for i in range(SLOTS)]
        bank_free = [sem(f"bank_free{i}") for i in range(BANKS)]
        (ones_ready, eps_ready, x_T, x_copied, param_T, param_ready, lb_step, lb_exp, ext_done, ext_ready, ext_stored, bias_stored, sp_met, pool_met,
         hi_ready, w_ready, value_tile_done, proj_done,
         sq_ready, sq_used, ss_done, rstd_step, rstd_ready, u_made, u_hi_ready, u_ready,
         link_hg, link_at, f_ready, lnf_ready, b_ready, eb_ready, sigf_step, sigf_ready, sigma_step, sigma_ready,
         q_ready, keys_ready, scores_done, kT_done, kT_ready, U_done, sT_ready, state_ready,
         O_done, osq_ready, osum_done, orstd_step, orstd_ready, y_made, y_hi_ready, y_ready,
         nat_done, res_done, nat_logits, res_logits, nat_probs, res_probs, bias_used,
         stat_a, stat_b, stat_back, merge_in, merge_exp, scaled, T_done, T_even, T_odd,
         fin_T, fin_base, fin_sq, fin_step, fin_rstd, fin_ready) = [sem(n) for n in (
             "ones_ready eps_ready x_T x_copied param_T param_ready lb_step lb_exp ext_done ext_ready ext_stored bias_stored sp_met pool_met "
             "hi_ready w_ready value_tile_done proj_done "
             "sq_ready sq_used ss_done rstd_step rstd_ready u_made u_hi_ready u_ready "
             "link_hg link_at f_ready lnf_ready b_ready eb_ready sigf_step sigf_ready sigma_step sigma_ready "
             "q_ready keys_ready scores_done kT_done kT_ready U_done sT_ready state_ready "
             "O_done osq_ready osum_done orstd_step orstd_ready y_made y_hi_ready y_ready "
             "nat_done res_done nat_logits res_logits nat_probs res_probs bias_used "
             "stat_a stat_b stat_back merge_in merge_exp scaled T_done T_even T_odd "
             "fin_T fin_base fin_sq fin_step fin_rstd fin_ready").split()]
        bias_loaded = [sem("bias_n_loaded"), sem("bias_r_loaded")]
        out_stored = [sem(f"out_stored{i}") for i in range(2 * ST)]

        def head(q, h):
            return q * HQ + h

        def quads(eng, body):
            with eng.Fori(0, NQ - 1) as q:
                body(q, False)
            body(NQ - 1, True)

        def wait_turn(eng, met, signal, value):
            eng.wait_ge(signal, value)
            eng.sem_inc(met, 1)

        def wait_emptied(eng, layer, q, e):
            _, bank, before = layer.event(q, e)
            eng.wait_ge(bank_free[bank], before + 1)

        def wait_tile_done(eng, layer, q, n, last):
            if q is None:
                kind, group, part = "value", n // 4, n % 4
                count, e = layer.value0 + 3 * group + part + 1, 4 * group + 3
            else:
                kind, group, part = layer.kind(n, last)
                count = layer.value0 + 3 * layer.groups * (q + 1) + 3 * group + part + 1
                e = {"head": n, "value": layer.heads + 4 * group + 3,
                     "out": layer.heads + (8 if last else layer.pro) + 2 * part + 1}[kind]
            if kind == "value" and part < 3:
                eng.wait_ge(value_tile_done, count)
            else:
                eng.wait_ge(proj_done, layer.event(q, e)[0] + 1)

        def value_bank(layer, q, e):
            if layer is AT and q is not None and e == layer.heads + ST - 1:
                return p_S[0]
            return proj[layer.event(q, e)[1]]

        def final_bank(t, half):
            return inner[t] if half == 0 else inner[ST] if t == 0 else proj[t - 1]

        FIRST_HALVES = ST * KT // 2
        def second_half(t):
            return FIRST_HALVES + (t + 1) * KT // 2

        block = ctx.enter_context(nc.Block())

        @block.sync
        def _(sp):
            def tile_source(layer, q, kind, group, part):
                if kind == "head":
                    cols = (HG_COLS if layer is HG else AT_COLS)[part]
                    return w_in[layer][:, :, ds(head(q, group) * P + cols, P)], KT
                if kind == "value":
                    col = (HG_VALUE if layer is HG else AT_VALUE)[group]
                    return w_in[layer][:, 2 * part:2 * part + 2, ds(q * (HQ * P) + col, HQ * P)], 2
                return w_out[layer][:, ds(q * HQ, HQ), part * 2 * P:(part + 1) * 2 * P], HQ

            def load(slot, source, k):
                sp.dma_start(raw[:, slot, :].rearrange("p (k n) -> p k n", k=k), source).then_inc(loaded[slot], 16)

            def load_after(layer, q, n, last):
                number, slot, _ = layer.tile(q, n)
                ahead = n + SLOTS
                if q is None:
                    where = (None, "value", ahead // 4, ahead % 4) if ahead < layer.pro else \
                        (0, *layer.kind(ahead - layer.pro, False))
                elif ahead < layer.quad_tiles(last):
                    what = layer.kind(ahead, last)
                    where = (q + 1 if what[0] == "value" else q, *what)
                elif not last:
                    where = (q + 1, *layer.kind(ahead - layer.T, False))
                elif layer is HG:
                    where, layer = (None, "value", 0, ahead - layer.quad_tiles(last)), AT
                else:
                    return
                wait_turn(sp, sp_met, w_ready, number + 1)
                load(slot, *tile_source(layer, 0 if where[0] is None else where[0], *where[1:]))

            for t in range(2):
                sp.dma_start(x_sb[:, 2 * t:2 * t + 2, :].rearrange("p a b -> p (a b)"), x_v[t]).then_inc(x_loaded[t], 16)
            sp.dma_start(ident[:, :], consts[:, 0:P]).then_inc(const_loaded[0], 16)
            sp.dma_start(prow[0:48, 0:P], hg_lb.rearrange("r (h p) -> (r h) p", p=P)).then_inc(const_loaded[1], 16)
            sp.dma_start(prow[48:64, 0:P], hg_norm.rearrange("r (h p) -> (r h) p", p=P)).then_inc(const_loaded[2], 16)
            sp.dma_start(prow[64:80, 0:P], ln_g.rearrange("r (h p) -> (r h) p", p=P)).then_inc(const_loaded[3], 16)
            for n in range(SLOTS):
                load(n, *tile_source(HG, 0, "value", 0, n))
            sp.dma_start(causal[:, :], consts[:, P:2 * P]).then_inc(const_loaded[4], 16)
            sp.dma_start(restart[:, :], consts[:, 2 * P:2 * P + S]).then_inc(const_loaded[4], 16)
            sp.dma_start(onehot_sb, onehot).then_inc(const_loaded[5], 16)
            sp.dma_start(relmask_sb, relmask).then_inc(const_loaded[6], 16)
            sp.dma_start(relb_sb, rel_bias).then_inc(const_loaded[7], 16)
            for t in range(2, ST):
                sp.wait_ge(x_T, KT * (t - 1))
                sp.dma_start(x_sb[:, 2 * (t % 2):2 * (t % 2) + 2, :].rearrange("p a b -> p (a b)"), x_v[t])\
                    .then_inc(x_loaded[t % 2], 16)
            sp.wait_ge(ext_ready, GROUPS)
            sp.dma_start(ext_dram.rearrange("g h e -> h g e"), ext_sb.rearrange("h (g e) -> h g e", g=GROUPS))\
                .then_inc(ext_stored, 16)
            for layer in (HG, AT):
                for n in range(layer.pro):
                    load_after(layer, None, n, False)

                def body(q, last):
                    for n in range(layer.quad_tiles(last)):
                        load_after(layer, q, n, last)
                quads(sp, body)
            sp.wait_ge(O_done, 2 * H)
            sp.dma_start(fg_bc, final_g.rearrange("(a d) -> a d", a=1).broadcast_to([P, D])).then_inc(const_loaded[0], 16)
            for i in range(2 * ST):
                sp.wait_ge(fin_ready, i + 1)
                sp.dma_start(out_v[i // 2, :, (i % 2) * S:(i % 2 + 1) * S], fin[i // 2][:, i % 2, :])\
                    .then_inc(out_stored[i], 16)
            for s in out_stored:
                sp.wait_ge(s, 16)
            sp.wait_ge(ext_stored, 16)

        @block.gpsimd
        def _(pool):
            nc.gpsimd.memset(ones[:, :], 1.0).then_inc(ones_ready, 1)
            def load_bias(g):
                pool.dma_start(bias_n[:, :], bias_dram[ds(g, 1), :, 0:2 * P].rearrange("a p n -> p (a n)"))\
                    .then_inc(bias_loaded[0], 16)
                pool.dma_start(bias_r[:, :, :], bias_dram[ds(g, 1), :, 2 * P:].rearrange("a p (k n) -> p (a k) n", k=2))\
                    .then_inc(bias_loaded[1], 16)

            pool.wait_ge(ext_stored, 16)
            for g, first, n in ((0, P - 1, 2 * P), (1, 2 * P - 1, P), (2, 2 * P - 1, P)):
                to = (0, 2 * P, 3 * P)[g]
                pool.dma_start(bias_dram[:, :, to:to + n],
                               bass.AP(ext_dram.tensor, g * H * EXT + first, [[EXT, H], [-1, P], [1, n]]))\
                    .then_inc(bias_stored, 16)
            pool.wait_ge(bias_stored, 16 * GROUPS)
            load_bias(0)

            def body(q, last):
                for h in range(HQ):
                    g = head(q, h)
                    if not (last and h == HQ - 1):
                        wait_turn(pool, pool_met, bias_used, 2 * g + 2)
                        load_bias(g + 1)
            quads(pool, body)

        @block.tensor
        def _(pe):
            def split_matmuls(bank, stationary, moving, first, last):
                ins = None
                for n, (a, b) in enumerate((("hi", "hi"), ("hi", "lo"), ("lo", "hi"))):
                    ins = nc.tensor.matmul(bank[:, :], stationary(a), moving(b),
                                           start=(first and n == 0), stop=(last and n == 2))
                return ins

            def open_bank(layer, q, e):
                _, bank, before = layer.event(q, e)
                if not (layer is HG and q is None and e < BANKS):
                    pe.wait_ge(bank_free[bank], before)
                return proj[bank]

            def head_tile(layer, q, n, half):
                number, slot, _ = layer.tile(q, n)
                event, bank, before = layer.event(q, n)
                if half == 0:
                    pe.wait_ge(w_ready, number + 1)
                    pe.wait_ge(bank_free[bank], before)
                for k in range(half * KT // 2, (half + 1) * KT // 2):
                    ins = split_matmuls(proj[bank], lambda a: w[a][:, slot, k * P:(k + 1) * P],
                                        lambda b: u[b][:, k, :], k == 0, k == KT - 1)
                if half:
                    ins.then_inc(proj_done, 1)

            def values(layer, q, group, s, half, wait_u=0):
                first = 4 * group + (0 if q is None else layer.heads)
                _, bank, before = layer.event(q, first + s)
                psum = value_bank(layer, q, first + s)
                if half == 0 and psum is proj[bank] and not (layer is HG and q is None and s < BANKS):
                    pe.wait_ge(bank_free[bank], before)
                for i in range(2 * half, 2 * half + 2):
                    number, slot, _ = layer.tile(q, first + i)
                    if s == 0:
                        pe.wait_ge(w_ready, number + 1)
                    for k in (2 * i, 2 * i + 1):
                        if wait_u and s == 0:
                            pe.wait_ge(u_ready, wait_u + k)
                        cols = slice(s, S, RES) if group else slice(s * P, (s + 1) * P)
                        ins = split_matmuls(psum, lambda a: u[a][:, k, cols],
                                            lambda b: w[b][:, slot, (k % 2) * S:(k % 2 + 1) * S], k == 0, k == KT - 1)
                    if i == 3:
                        ins.then_inc(proj_done, 1)
                    elif s == ST - 1:
                        ins.then_inc(value_tile_done, 1)

            def out_column(layer, q, tile, event, c, heads):
                number, slot, _ = layer.tile(q, tile)
                _, bank, before = layer.event(q, event)
                pe.wait_ge(w_ready, number + 1)
                pe.wait_ge(bank_free[bank], before)
                for k in heads:
                    if c == 0:
                        pe.wait_ge(y_ready, (0 if layer is HG else H) + head(q, k) + 1)
                    at = (2 * k + c % 2) * P
                    ins = split_matmuls(proj[bank], lambda a: w[a][:, slot, at:at + P],
                                        lambda b: y[b][:, k, :], k == heads[0], k == heads[-1])
                ins.then_inc(proj_done, 1)

            def final_transposes(k):
                wait_emptied(pe, AT, NQ - 1, AT.heads + KT + k)
                for t in range(ST if k < KT // 2 else 1):
                    final_transpose(t, k)
                if k == KT - 1:
                    for t in range(1, ST):
                        for kk in range(KT // 2, KT):
                            final_transpose(t, kk)

            def final_transpose(t, k):
                nc.tensor.transpose(final_bank(t, k // 4)[:, (k % 4) * P:(k % 4 + 1) * P],
                                    hT[:, k, t * P:(t + 1) * P], ident[:, :]).then_inc(fin_T, 1)

            def out_projection(layer, q, last):
                tile = layer.heads + (0 if last else layer.pro)
                for c in range(KT):
                    out_column(layer, q, tile + c // 2, tile + c + (KT if last else 0), c, (HQ - 1,) if last else range(HQ))
                    if layer is AT and last and c >= 2:
                        final_transposes(c - 2)

            def sum_squares(first):
                for k in range(KT):
                    pe.wait_ge(sq_ready, first + k + 1)
                    nc.tensor.matmul(p_ss[:, :], ones[:, :], tmp[:, k % 2, :],
                                     start=(k == 0), stop=(k == KT - 1)).then_inc(ss_done, 1)

            pe.wait_ge(ones_ready, 1)
            pe.wait_ge(const_loaded[0], 16)
            for t in range(ST):
                pe.wait_ge(x_loaded[t % 2], 16 * (t // 2 + 1))
                for k in range(KT):
                    i = t * KT + k
                    if i >= 4 and i % 4 == 0:
                        pe.wait_ge(x_copied, i // 4 - (0 if i < 8 else 1))
                    nc.tensor.transpose(inner[(i // 4) % 2][:, (i % 4) * P:(i % 4 + 1) * P],
                                        x_sb[:, 2 * (t % 2) + k // 4, (k % 4) * P:(k % 4 + 1) * P],
                                        ident[:, :]).then_inc(x_T, 1)
                if t == 0:
                    for i in (1, 2, 3):
                        pe.wait_ge(const_loaded[i], 16)
                    nc.tensor.transpose(inner[2][:, 0:80], prow[0:80, 0:P], ident[0:80, 0:80]).then_inc(param_T, 1)
                    pe.wait_ge(param_ready, 1)
                    pe.wait_ge(const_loaded[5], 16)
                    pe.wait_ge(const_loaded[7], 16)
                    for g in range(GROUPS):
                        if g:
                            pe.wait_ge(ext_ready, g)
                        nc.tensor.matmul(inner[2][0:H, 0:EXT], relb_sb[:, g * H:(g + 1) * H],
                                         onehot_sb[:, g * EXT:(g + 1) * EXT], start=True, stop=True)\
                            .then_inc(ext_done, 1)
            sum_squares(0)

            for s in range(ST):
                for half in range(2):
                    values(HG, None, 0, s, half, wait_u=1)
            wait_emptied(pe, HG, None, HG.pro - 1)

            def scores(g):
                pe.wait_ge(q_ready, g + 1)
                pe.wait_ge(keys_ready, g + 1)
                for b in range(ST):
                    for j in range(NC):
                        ins = nc.tensor.matmul(p_sc[:, b * P + j * CH:b * P + (j + 1) * CH], keys[:, b, j, :],
                                               qd[:, b * P + j * CH:b * P + (j + 1) * CH], start=True, stop=True)
                ins.then_inc(scores_done, 1)
                for b in range(ST - 1):
                    ins = nc.tensor.transpose(p_kT[:, b * P:(b + 1) * P], keys[:, b, NC, :], ident[:, :])
                ins.then_inc(kT_done, 1)

            def updates(g, h):
                pe.wait_ge(kT_ready, g + 1)
                for b in range(ST - 1):
                    ins = nc.tensor.matmul(p_U[:, b * P:(b + 1) * P], kT[:, b, :], v_sb[0][:, b, h * P:(h + 1) * P],
                                           start=True, stop=True)
                ins.then_inc(U_done, 1)

            def outputs(g, h):
                pe.wait_ge(sT_ready, g + 1)
                pe.wait_ge(state_ready, g + 1)
                for b in range(ST):
                    s = slice(b * P, (b + 1) * P)
                    ins = nc.tensor.matmul(p_O[:, s], v_sb[0][:, b, h * P:(h + 1) * P], sT[:, s],
                                           start=True, stop=(b == 0))
                    if b:
                        ins = nc.tensor.matmul(p_O[:, s], state[:, b - 1, :], qs[:, s], start=False, stop=True)
                ins.then_inc(O_done, 1)

            def norm_sum(g):
                pe.wait_ge(osq_ready, g + 1)
                nc.tensor.matmul(p_ss[:, :], ones[:, :], enb[:, :], start=True, stop=True).then_inc(osum_done, 1)

            def recurrence(g, h, half):
                if half == 0:
                    scores(g)
                elif half == 1:
                    updates(g, h)
                elif half == 2:
                    outputs(g, h)
                elif half == 3:
                    norm_sum(g)

            def hg_body(q, last):
                for h in range(HQ):
                    for half in range(2 * HG.per_head):
                        head_tile(HG, q, HG.per_head * h + half // 2, half % 2)
                        if h:
                            recurrence(head(q, h - 1), h - 1, half)
                for half in range(KT):
                    if last:
                        out_column(HG, q, HG.heads + half // 2, HG.heads + half, half, range(HQ - 1))
                    else:
                        values(HG, q, 0, half // 2, half % 2)
                    recurrence(head(q, HQ - 1), HQ - 1, half)
                out_projection(HG, q, last)
                if not last:
                    wait_emptied(pe, HG, q, HG.heads + HG.pro - 1)
            quads(pe, hg_body)

            sum_squares(KT)
            for g in range(GROUPS):
                for s in range(ST):
                    for half in range(2):
                        values(AT, None, g, s, half, wait_u=0 if g else KT + 1)
            wait_emptied(pe, AT, None, AT.pro - 1)

            def natural_logits(q, h):
                wait_emptied(pe, AT, q, 7 * h + K0)
                for b in range(ST):
                    lo = max(b - 1, 0) * P
                    n = (b + 1) * P - lo
                    bank = p_S[b // 2]
                    at = (b % 2) * 2 * P
                    ins = nc.tensor.matmul(bank[:, at:at + n], qk[:, 0, b * P:(b + 1) * P], qk[:, 1, lo:lo + n],
                                           start=True, stop=True)
                    if b % 2:
                        ins.then_inc(nat_done, 1)

            def residue_logits(g, q, h):
                wait_emptied(pe, AT, q, 7 * h + K2)
                pe.wait_ge(nat_logits, g + 1)
                for r in range(RES):
                    for i in range(2):
                        s = slice(r * P, (r + 1) * P)
                        ins = nc.tensor.matmul(p_S[r // 2][:, ((r % 2) * 2 + i) * P:((r % 2) * 2 + i + 1) * P],
                                               qk[:, 2 + 2 * i, s], qk[:, 3 + 2 * i, s], start=True, stop=True)
                    if r % 2:
                        ins.then_inc(res_done, 1)

            def transposes(g, batches):
                for n in batches:
                    if n < 2:
                        pe.wait_ge(scaled, 2 * g + n + 1)
                    if n == 2:
                        pe.wait_ge(T_even, 2 * g + 1)
                    if n == 3:
                        pe.wait_ge(T_odd, 2 * g + 1)
                    for i in BATCHES[n]:
                        b, c = TILES[i]
                        if i < NATURAL:
                            src = probs[:, b, (c - b + 1 if b else 0) * P:(c - b + 2 if b else 1) * P]
                        else:
                            src = probs[:, ST + b, (c - 1) * P:c * P]
                        ins = nc.tensor.transpose(p_T[n % 2][:, (i % 4) * P:(i % 4 + 1) * P], src, ident[:, :])
                    ins.then_inc(T_done, 1)

            def attend(g, h):
                pe.wait_ge(T_even, 2 * g + 2)
                pe.wait_ge(T_odd, 2 * g + 2)
                for i, (b, c) in enumerate(TILES):
                    if i < NATURAL:
                        vals, o = v_sb[0][:, c, h * P:(h + 1) * P], p_O[:, b * P:(b + 1) * P]
                    else:
                        vals, o = v_sb[c][:, b, h * P:(h + 1) * P], p_O[:, b::RES]
                    ins = nc.tensor.matmul(o, vals, pT[:, i, :], start=(i == 0), stop=(i == len(TILES) - 1),
                                           skip_group_check=True)
                ins.then_inc(O_done, 1)

            def attention(g, h, half):
                if half == 3:
                    transposes(g, (0, 1))
                elif half == 4:
                    transposes(g, (2, 3))
                elif half == 5:
                    attend(g, h)

            def at_body(q, last):
                for h in range(HQ):
                    for half in range(2 * AT.per_head):
                        head_tile(AT, q, AT.per_head * h + half // 2, half % 2)
                        if h:
                            attention(head(q, h - 1), h - 1, half - 1)
                        if half == 2 * K1:
                            natural_logits(q, h)
                        elif half == 2 * GA:
                            residue_logits(head(q, h), q, h)
                for half in range(KT if last else 2 * AT.pro):
                    if last:
                        out_column(AT, q, AT.heads + half // 2, AT.heads + half, half, range(HQ - 1))
                        attention(head(q, HQ - 1), HQ - 1, half - 2)
                    else:
                        if half == 2 * (ST - 1):
                            pe.wait_ge(res_logits, head(q, HQ - 1) + 1)
                        values(AT, q, half // 8, half // 2 % 4, half % 2)
                        attention(head(q, HQ - 1), HQ - 1, half - 1)
                out_projection(AT, q, last)
                if not last:
                    wait_emptied(pe, AT, q, AT.heads + AT.pro - 1)
            quads(pe, at_body)

            final_transposes(KT - 2)
            final_transposes(KT - 1)

        @block.scalar
        def _(act):
            def split_hi(layer, q, n, last):
                number, slot, use = layer.tile(q, n)
                if layer is AT and last and n + SLOTS >= layer.quad_tiles(True):
                    return
                act.wait_ge(loaded[slot], use * 16 + 32)
                wait_tile_done(act, layer, q, n, last)
                nc.scalar.activation(w["hi"][:, slot, :], raw[:, slot, :], ACT.Copy).then_inc(hi_ready, 1)

            def copy_values(layer, q, group, e):
                _, bank, _ = layer.event(q, e)
                number = layer.event(q, e)[0]
                act.wait_ge(proj_done, number + 1)
                nc.scalar.activation(v_sb[group][:, (e - (0 if q is None else layer.heads)) % ST, :],
                                     value_bank(layer, q, e)[:, :], ACT.Copy).then_inc(bank_free[bank], 1)

            def norm(which):
                for k in range(KT):
                    if which:
                        wait_emptied(act, HG, NQ - 1, HG.heads + KT + k)
                    else:
                        act.wait_ge(x_copied, 2 * ST)
                    if k >= 2:
                        act.wait_ge(ss_done, which * KT + k - 1)
                    nc.scalar.activation(tmp[:, k % 2, :], hT[:, k, :], ACT.Square).then_inc(sq_ready, 1)
                act.wait_ge(ss_done, which * KT + KT)
                nc.scalar.activation(rstd[:, :], p_ss[:, :], ACT.Ln, scale=1.0 / D, bias=eps[:, :]).then_inc(rstd_step, 1)
                act.wait_ge(rstd_step, which + 1)
                nc.scalar.activation(rstd[:, :], rstd[:, :], ACT.Exp, scale=-0.5).then_inc(rstd_ready, 1)
                for k in range(KT):
                    act.wait_ge(u_made, which * KT + k + 1)
                    nc.scalar.activation(u["hi"][:, k, :], tmp[:, k % 2, :], ACT.Copy).then_inc(u_hi_ready, 1)

            nc.scalar.preload_act_table_set("natural_log_exp_and_others")
            act.wait_ge(eps_ready, 1)
            for n in range(SLOTS):
                act.wait_ge(loaded[n], 16)
                nc.scalar.activation(w["hi"][:, n, :], raw[:, n, :], ACT.Copy).then_inc(hi_ready, 1)
            act.wait_ge(lb_step, 3)
            nc.scalar.activation(param[:, 0:3 * H], param[:, 0:3 * H], ACT.Exp).then_inc(lb_exp, 1)
            norm(0)
            def value_events(layer, q, group, first):
                base = 4 * group + (0 if q is None else layer.heads)
                for s in range(first, ST):
                    if s == ST - 1:
                        for i in range(3):
                            split_hi(layer, q, base + i, False)
                    copy_values(layer, q, group, base + s)
                split_hi(layer, q, base + 3, False)

            value_events(HG, None, 0, 0)

            def kT_copy(g):
                act.wait_ge(kT_done, g + 1)
                nc.scalar.activation(kT[:, :, :].rearrange("p a b -> p (a b)"), p_kT[:, 0:(ST - 1) * P], ACT.Copy)\
                    .then_inc(kT_ready, 1)

            def square(g):
                act.wait_ge(O_done, g + 1)
                nc.scalar.activation(enb[:, :], p_O[:, :], ACT.Square).then_inc(osq_ready, 1)

            def out_rstd(g):
                act.wait_ge(osum_done, g + 1)
                nc.scalar.activation(rstd[:, :], p_ss[:, :], ACT.Ln, scale=1.0 / P, bias=eps[:, :]).then_inc(orstd_step, 1)
                act.wait_ge(orstd_step, g + 1)
                nc.scalar.activation(rstd[:, :], rstd[:, :], ACT.Exp, scale=-0.5).then_inc(orstd_ready, 1)

            def y_high(g, slot):
                act.wait_ge(y_made, g + 1)
                nc.scalar.activation(y["hi"][:, slot, :], y_f[:, :], ACT.Copy).then_inc(y_hi_ready, 1)

            def sigmoid(g):
                act.wait_ge(sigma_step, 2 * g + 1)
                nc.scalar.activation(eg[:, :], eg[:, :], ACT.Ln, bias=ones[:, 0:1]).then_inc(sigma_step, 1)
                act.wait_ge(sigma_step, 2 * g + 2)
                nc.scalar.activation(eg[:, :], eg[:, :], ACT.Exp, scale=-1.0).then_inc(sigma_ready, 1)

            def hg_body(q, last):
                for h in range(HQ):
                    g, before = head(q, h), head(q, h - 1) if h else None
                    number, bank, _ = HG.event(q, 3 * h + F_)
                    if h:
                        kT_copy(before)
                    act.wait_ge(proj_done, number + 1)
                    nc.scalar.activation(ef[:, :], proj[bank][:, :], ACT.Exp, scale=-1.0).then_inc(bank_free[bank], 1)
                    wait_emptied(act, HG, q, 3 * h + F_)
                    nc.scalar.activation(ef[:, :], ef[:, :], ACT.Ln, bias=ones[:, 0:1]).then_inc(sigf_step, 1)
                    act.wait_ge(sigf_step, g + 1)
                    nc.scalar.activation(ef[:, :], ef[:, :], ACT.Exp, scale=-1.0).then_inc(sigf_ready, 1)
                    split_hi(HG, q, 3 * h + F_, last)
                    act.wait_ge(f_ready, g + 1)
                    nc.scalar.activation(lnf[:, :], fg[:, :], ACT.Ln).then_inc(lnf_ready, 1)
                    if h:
                        square(before)
                    act.wait_ge(b_ready, g + 1)
                    nc.scalar.activation(eb[:, :], bb[:, :], ACT.Exp).then_inc(eb_ready, 1)
                    if h:
                        out_rstd(before)
                    nc.scalar.activation(enb[:, :], bb[:, :], ACT.Exp, scale=-1.0).then_inc(eb_ready, 1)
                    split_hi(HG, q, 3 * h + Q_, last)
                    if h:
                        y_high(before, h - 1)
                    number, bank, _ = HG.event(q, 3 * h + G_)
                    act.wait_ge(proj_done, number + 1)
                    nc.scalar.activation(eg[:, :], proj[bank][:, :], ACT.Exp, scale=-1.0).then_inc(sigma_step, 1)
                    split_hi(HG, q, 3 * h + G_, last)
                    sigmoid(g)
                g = head(q, HQ - 1)
                kT_copy(g)
                square(g)
                if not last:
                    copy_values(HG, q, 0, HG.heads)
                    copy_values(HG, q, 0, HG.heads + 1)
                out_rstd(g)
                y_high(g, HQ - 1)
                if not last:
                    value_events(HG, q, 0, 2)
                for n in range(HG.quad_tiles(last) - 4, HG.quad_tiles(last)):
                    split_hi(HG, q, n, last)
            quads(act, hg_body)

            norm(1)
            for g in range(GROUPS):
                value_events(AT, None, g, 0)

            def exps(g, first, logits, signal):
                act.wait_ge(logits, g + 1)
                for b in range(ST):
                    i = first + b
                    n = P if i == 0 else 2 * P
                    nc.scalar.activation(probs[:, i, 0:n], probs[:, i, 0:n], ACT.Exp, bias=negm[:, i:i + 1],
                                         accum_out=stat[:, i // ST, 1, b:b + 1]).then_inc(signal, 1)

            natural = [d.rearrange("k (b p) -> p (k b)", p=P) for d in (nat_dram, res_dram)]
            residue = [d.rearrange("k (i r) -> i k r", r=RES) for d in (nat_dram, res_dram)]

            def store_natural(g):
                act.wait_ge(nat_probs, 4 * g + 4)
                act.dma_start(natural[0], stat[:, 0, :, :].rearrange("p k b -> p (k b)"),
                              allow_slow_non_contiguous=True).then_inc(stat_a, 16)

            def load_natural(g):
                act.wait_ge(stat_a, 32 * g + 16)
                act.dma_start(stat_o[:, 1, :, :], residue[0]).then_inc(stat_a, 16)

            def store_residue(g):
                act.wait_ge(res_probs, 4 * g + 4)
                act.dma_start(residue[1], stat[:, 1, :, :]).then_inc(stat_b, 16)

            def load_residue(g):
                act.wait_ge(stat_b, 32 * g + 16)
                act.dma_start(stat_o[:, 0, :, :].rearrange("p k b -> p (k b)"), natural[1],
                              allow_slow_non_contiguous=True).then_inc(stat_b, 16)

            def merge_exps(g):
                act.wait_ge(merge_in, g + 1)
                nc.scalar.activation(merge[:, :, :, :], both[:, :, :, :], ACT.Exp).then_inc(merge_exp, 1)

            def copy_odd(g):
                for n, b in enumerate((1, 3)):
                    act.wait_ge(T_done, 4 * g + b + 1)
                    nc.scalar.activation(pT[:, BATCHES[b][0]:BATCHES[b][-1] + 1, :],
                                         p_T[1][:, 0:len(BATCHES[b]) * P].rearrange("p (a b) -> p a b", b=P),
                                         ACT.Copy).then_inc(T_odd, 1)

            def at_body(q, last):
                for h in range(HQ):
                    g, before = head(q, h), head(q, h - 1) if h else None
                    for i in range(7):
                        number, bank, _ = AT.event(q, 7 * h + i)
                        if i == K0 and h:
                            merge_exps(before)
                        if i == Q1 and h:
                            copy_odd(before)
                        if i == K1 and h:
                            y_high(before + H, h - 1)
                        if i == K1:
                            exps(g, 0, nat_logits, nat_probs)
                        if i == GA:
                            load_natural(g)
                            exps(g, ST, res_logits, res_probs)
                            split_hi(AT, q, 7 * h + i, last)
                            store_residue(g)
                        act.wait_ge(proj_done, number + 1)
                        if i == GA:
                            nc.scalar.activation(eg[:, :], proj[bank][:, :], ACT.Exp, scale=-1.0).then_inc(sigma_step, 1)
                            sigmoid(H + g)
                        else:
                            o, src = qk[:, i, :], proj[bank][:, :]
                            if i >= Q1:
                                o = qk[:, i, :].rearrange("p (r i) -> p r i", r=RES)
                                src = proj[bank][:, :].rearrange("p (i r) -> p r i", r=RES)
                            nc.scalar.activation(o, src, ACT.Copy, scale=QSCALE if i in (Q0, Q1, Q2) else 1.0)\
                                .then_inc(bank_free[bank], 1)
                            split_hi(AT, q, 7 * h + i, last)
                        if i == K1:
                            store_natural(g)
                    load_residue(g)
                g = head(q, HQ - 1)
                merge_exps(g)
                copy_odd(g)
                if not last:
                    split_hi(AT, q, AT.heads, False)
                    act.wait_ge(O_done, H + g + 1)
                    copy_values(AT, q, 0, AT.heads)
                y_high(g + H, HQ - 1)
                if not last:
                    copy_values(AT, q, 0, AT.heads + 1)
                    split_hi(AT, q, AT.heads + 1, False)
                    copy_values(AT, q, 0, AT.heads + 2)
                    split_hi(AT, q, AT.heads + 2, False)
                    copy_values(AT, q, 0, AT.heads + 3)
                    split_hi(AT, q, AT.heads + 3, False)
                    for group in range(1, GROUPS):
                        value_events(AT, q, group, 0)
                for n in range(AT.quad_tiles(last) - 4, AT.quad_tiles(last)):
                    split_hi(AT, q, n, last)
            quads(act, at_body)

            act.wait_ge(fin_T, FIRST_HALVES)
            for t in range(ST):
                nc.scalar.activation(raw[:, t, 0:S], final_bank(t, 0)[:, :], ACT.Square,
                                     accum_out=cols[:, t:t + 1]).then_inc(fin_sq, 1)
            act.wait_ge(fin_base, 1)
            for t in range(ST):
                act.wait_ge(fin_T, second_half(t))
                nc.scalar.activation(raw[:, t, S:2 * S], final_bank(t, 1)[:, :], ACT.Square,
                                     accum_out=cols[:, 4 + t:5 + t]).then_inc(fin_sq, 1)
                act.wait_ge(fin_sq, ST + t + 1)
                nc.scalar.activation(cols[:, 8 + t:9 + t], cols[:, 4 + t:5 + t], ACT.Ln, scale=1.0 / D,
                                     bias=cols[:, t:t + 1]).then_inc(fin_step, 1)
                act.wait_ge(fin_step, t + 1)
                nc.scalar.activation(cols[:, 12 + t:13 + t], cols[:, 8 + t:9 + t], ACT.Exp, scale=-0.5).then_inc(fin_rstd, 1)

        @block.vector
        def _(dve):
            def split_lo(layer, q, n, last):
                if layer is AT and last and n + SLOTS >= layer.quad_tiles(True):
                    return
                number, slot, _ = layer.tile(q, n)
                dve.wait_ge(hi_ready, number + SLOTS + 1)
                nc.vector.tensor_tensor(w["lo"][:, slot, :], raw[:, slot, :], w["hi"][:, slot, :].bitcast(F32),
                                        ALU.subtract).then_inc(w_ready, 1)

            def norm(which):
                dve.wait_ge(rstd_ready, which + 1)
                for k in range(KT + 1):
                    if k < KT:
                        if k >= 2:
                            dve.wait_ge(u_ready, which * KT + k - 1)
                        nc.vector.scalar_tensor_tensor(out=tmp[:, k % 2, :], in0=hT[:, k, :],
                                                       scalar=param[:, 64 + which * KT + k:65 + which * KT + k],
                                                       in1=rstd[:, :], op0=ALU.mult, op1=ALU.mult).then_inc(u_made, 1)
                    if k:
                        dve.wait_ge(u_hi_ready, which * KT + k)
                        nc.vector.tensor_tensor(u["lo"][:, k - 1, :], tmp[:, (k - 1) % 2, :],
                                                u["hi"][:, k - 1, :].bitcast(F32), ALU.subtract).then_inc(u_ready, 1)

            nc.vector.memset(eps[:, :], EPS).then_inc(eps_ready, 1)
            for i in range(2 * ST):
                t, half = i // 2, i % 2
                dve.wait_ge(x_T, 4 * i + 4)
                nc.vector.tensor_copy(hT[:, 4 * half:4 * half + 4, t * P:(t + 1) * P],
                                      inner[i % 2][:, :].rearrange("p (a b) -> p a b", b=P)).then_inc(x_copied, 1)
                if i == 1:
                    dve.wait_ge(param_T, 1)
                    nc.vector.tensor_copy(param[:, :], inner[2][:, 0:80]).then_inc(param_ready, 1)
                    dve.wait_ge(param_ready, 1)
                    nc.vector.tensor_tensor(lb[:, :], param[:, 0:H], param[:, H:2 * H], ALU.max).then_inc(lb_step, 1)
                    dve.wait_ge(lb_step, 1)
                    nc.vector.tensor_tensor(oml[:, :], lb[:, :], param[:, 2 * H:3 * H], ALU.max).then_inc(lb_step, 1)
                    dve.wait_ge(lb_step, 2)
                    for r in range(3):
                        ins = nc.vector.tensor_tensor(param[:, r * H:(r + 1) * H], param[:, r * H:(r + 1) * H],
                                                      oml[:, :], ALU.subtract)
                    ins.then_inc(lb_step, 1)
                    dve.wait_ge(const_loaded[6], 16)
                    for g in range(GROUPS):
                        dve.wait_ge(ext_done, g + 1)
                        nc.vector.tensor_tensor(ext_sb[:, g * EXT:(g + 1) * EXT], inner[2][0:H, 0:EXT],
                                                relmask_sb[:, g * EXT:(g + 1) * EXT], ALU.add).then_inc(ext_ready, 1)
            for n in range(SLOTS):
                dve.wait_ge(hi_ready, n + 1)
                nc.vector.tensor_tensor(w["lo"][:, n, :], raw[:, n, :], w["hi"][:, n, :].bitcast(F32),
                                        ALU.subtract).then_inc(w_ready, 1)
            dve.wait_ge(lb_exp, 1)
            steps = 3

            def step(ins):
                nonlocal steps
                steps += 1
                ins.then_inc(lb_step, 1)
                dve.wait_ge(lb_step, steps)

            step(nc.vector.tensor_tensor(lb[:, :], param[:, 0:H], param[:, H:2 * H], ALU.add))
            step(nc.vector.tensor_tensor(oml[:, :], lb[:, :], param[:, 2 * H:3 * H], ALU.add))
            step(nc.vector.reciprocal(oml[:, :], oml[:, :]))
            step(nc.vector.tensor_tensor(lb[:, :], param[:, 0:H], oml[:, :], ALU.mult))
            step(nc.vector.tensor_scalar(oml[:, :], lb[:, :], -1.0, 1.0, ALU.mult, ALU.add))
            norm(0)
            dve.wait_ge(ext_stored, 16)
            step(nc.vector.memset(keys[:, :, :, :], 0.0))
            step(nc.vector.memset(dec[:, :, :], 1.0))
            dve.wait_ge(const_loaded[4], 32)
            for n in range(HG.pro):
                split_lo(HG, None, n, False)

            def gate(layer, q, h, g, event):
                _, bank, _ = layer.event(q, event)
                dve.wait_ge(sigma_ready, g + 1)
                nc.vector.tensor_tensor(sg[:, :], proj[bank][:, :], eg[:, :], ALU.mult).then_inc(bank_free[bank], 1)

            def mask_scores(g):
                dve.wait_ge(scores_done, g + 1)
                nc.vector.tensor_tensor(sT[:, :].rearrange("p (b c) -> p b c", b=ST),
                                        p_sc[:, :].rearrange("p (b c) -> p b c", b=ST),
                                        causal[:, :].unsqueeze(1).broadcast_to([P, ST, P]), ALU.mult)\
                    .then_inc(sT_ready, 1)

            def states(link, g):
                dve.wait_ge(U_done, g + 1)
                link(nc.vector.tensor_copy(state[:, 0, :], p_U[:, 0:P]))
                link(nc.vector.scalar_tensor_tensor(out=state[:, 1, :], in0=state[:, 0, :], scalar=dec[:, 1, NC:NC + 1],
                                                    in1=p_U[:, P:2 * P], op0=ALU.mult, op1=ALU.add))
                nc.vector.scalar_tensor_tensor(out=state[:, 2, :], in0=state[:, 1, :], scalar=dec[:, 2, NC:NC + 1],
                                               in1=p_U[:, 2 * P:3 * P], op0=ALU.mult, op1=ALU.add)\
                    .then_inc(state_ready, 1)

            def forget(g):
                dve.wait_ge(sigf_ready, g + 1)
                nc.vector.tensor_scalar(fg[:, :], ef[:, :], oml[:, ds(g, 1)], lb[:, ds(g, 1)], ALU.mult, ALU.add)\
                    .then_inc(f_ready, 1)
                dve.wait_ge(f_ready, g + 1)
                nc.vector.tensor_scalar(kk[:, :], fg[:, :], -1.0, 1.0, ALU.mult, ALU.add)

            def cumulate(g):
                dve.wait_ge(lnf_ready, g + 1)
                nc.vector.tensor_tensor_scan(bb[:, :], restart[:, :], lnf[:, :], 0.0, ALU.mult, ALU.add)\
                    .then_inc(b_ready, 1)

            def decays(link, q, h, g):
                number, bank, _ = HG.event(q, 3 * h + Q_)
                chunk = lambda t: t[:, :].rearrange("p (b j c) -> p b j c", b=ST, j=NC)
                A = chunk(eb)[:, :, :, CH - 1:CH]
                dve.wait_ge(proj_done, number + 1)
                dve.wait_ge(eb_ready, 2 * g + 2)
                nc.vector.tensor_tensor(qd[:, :], proj[bank][:, :], eb[:, :], ALU.mult).then_inc(bank_free[bank], 1)
                flat = keys[:, :, :, :].rearrange("p b s k -> p b (s k)")
                own = bass.AP(flat.tensor, flat.offset, [list(flat.ap[0]), [(NC + 1) * P, ST], [P + CH, NC], [1, CH]])
                after = bass.AP(flat.tensor, flat.offset + P, [list(flat.ap[0]), [(NC + 1) * P, ST], [P + CH, NC], [1, CH]])
                link(nc.vector.tensor_tensor(own, chunk(kk), chunk(enb), ALU.mult))
                link(nc.vector.tensor_tensor(after, own, A.broadcast_to([P, ST, NC, CH]), ALU.mult))
                link(nc.vector.tensor_copy(dec[:, :, 1:2], A[:, :, 0, :]))
                for j in range(1, NC):
                    link(nc.vector.tensor_tensor(dec[:, :, j + 1:j + 2], dec[:, :, j:j + 1], A[:, :, j, :], ALU.mult))
                    ins = nc.vector.tensor_tensor(keys[:, :, j + 1, 0:j * CH], keys[:, :, j, 0:j * CH],
                                                  A[:, :, j, :].broadcast_to([P, ST, j * CH]), ALU.mult)
                    if j < NC - 1:
                        link(ins)
                    else:
                        ins.then_inc(keys_ready, 1)
                nc.vector.tensor_tensor(chunk(qs), chunk(qd), dec[:, :, 0:NC].unsqueeze(3).broadcast_to([P, ST, NC, CH]),
                                        ALU.mult).then_inc(q_ready, 1)

            def hg_output(link, g, slot):
                dve.wait_ge(orstd_ready, g + 1)
                link(nc.vector.tensor_tensor(y_f[:, :], p_O[:, :], rstd[:, :], ALU.mult))
                nc.vector.scalar_tensor_tensor(out=y_f[:, :], in0=y_f[:, :], scalar=param[:, ds(g + 3 * H, 1)],
                                               in1=sg[:, :], op0=ALU.mult, op1=ALU.mult).then_inc(y_made, 1)

            def y_low(g, slot):
                dve.wait_ge(y_hi_ready, g + 1)
                nc.vector.tensor_tensor(y["lo"][:, slot, :], y_f[:, :], y["hi"][:, slot, :].bitcast(F32), ALU.subtract)\
                    .then_inc(y_ready, 1)

            def add_out(layer, q, event, k):
                number, bank, _ = layer.event(q, event)
                dve.wait_ge(proj_done, number + 1)
                nc.vector.tensor_tensor(hT[:, k, :], hT[:, k, :], proj[bank][:, :], ALU.add)\
                    .then_inc(bank_free[bank], 1)

            def out_shares(layer, q, last):
                tile = layer.heads + (0 if last else layer.pro)
                for i in range(4):
                    for c in (2 * i, 2 * i + 1):
                        add_out(layer, q, tile + c + (KT if last else 0), c)
                    split_lo(layer, q, tile + i, last)

            def hg_body(q, last):
                links = 0

                def link(ins):
                    nonlocal links
                    links += 1
                    ins.then_inc(link_hg, 1)
                    dve.wait_ge(link_hg, q * LINKS_HG + links)

                for h in range(HQ):
                    g, before = head(q, h), head(q, h - 1) if h else None
                    if h:
                        gate(HG, q, h - 1, before, 3 * (h - 1) + G_)
                        mask_scores(before)
                        states(link, before)
                    forget(g)
                    cumulate(g)
                    split_lo(HG, q, 3 * h + F_, last)
                    if h:
                        hg_output(link, before, h - 1)
                    decays(link, q, h, g)
                    split_lo(HG, q, 3 * h + Q_, last)
                    if h:
                        y_low(before, h - 1)
                    split_lo(HG, q, 3 * h + G_, last)
                g = head(q, HQ - 1)
                gate(HG, q, HQ - 1, g, 3 * (HQ - 1) + G_)
                if last:
                    add_out(HG, q, HG.heads, 0)
                mask_scores(g)
                if last:
                    add_out(HG, q, HG.heads + 1, 1)
                states(link, g)
                if last:
                    for k in (2, 3):
                        add_out(HG, q, HG.heads + k, k)
                hg_output(link, g, HQ - 1)
                y_low(g, HQ - 1)
                if last:
                    for k in range(4, KT):
                        add_out(HG, q, HG.heads + k, k)
                else:
                    for n in range(4):
                        split_lo(HG, q, HG.heads + n, last)
                out_shares(HG, q, last)
                assert links == LINKS_HG, links
            quads(dve, hg_body)

            norm(1)
            for n in range(AT.pro):
                split_lo(AT, None, n, False)

            def biases(g, first, tile, done, loaded_, banks, signal, link):
                dve.wait_ge(loaded_, 16 * g + 16)
                for i in range(2):
                    dve.wait_ge(done, 2 * g + i + 1)
                    if first == 0 and i == 0:
                        nc.vector.tensor_tensor(probs[:, 0, 0:P], banks[0][:, 0:P], tile[:, P:2 * P], ALU.add)
                        ins = nc.vector.tensor_tensor(probs[:, 1, :], banks[0][:, 2 * P:4 * P], tile, ALU.add)
                    else:
                        ins = nc.vector.tensor_tensor(probs[:, first + 2 * i:first + 2 * i + 2, :],
                                                      banks[i][:, :].rearrange("p (a b) -> p a b", a=2),
                                                      tile.unsqueeze(1).broadcast_to([P, 2, 2 * P]), ALU.add)
                ins.then_inc(bias_used, 1)
                dve.wait_ge(bias_used, 2 * g + (2 if first else 1))
                if first == 0:
                    nc.vector.tensor_reduce(stat[:, 0, 0, 0:1], probs[:, 0, 0:P], AX.X, ALU.max)
                    link(nc.vector.tensor_reduce(stat[:, 0, 0, 1:ST], probs[:, 1:ST, :], AX.X, ALU.max))
                else:
                    link(nc.vector.tensor_reduce(stat[:, 1, 0, :], probs[:, ST:2 * ST, :], AX.X, ALU.max))
                nc.vector.tensor_scalar(negm[:, first:first + ST], stat[:, first // ST, 0, :], -1.0, None, ALU.mult)\
                    .then_inc(signal, 1)

            def merge_and_scale(link, g):
                dve.wait_ge(stat_a, 32 * g + 32)
                dve.wait_ge(stat_b, 32 * g + 32)
                link(nc.vector.tensor_tensor(share[:, :, :], stat[:, :, 0, :], stat_o[:, :, 0, :], ALU.max))
                nc.vector.tensor_tensor(both[:, 0, :, :], stat[:, :, 0, :], share[:, :, :], ALU.subtract)
                nc.vector.tensor_tensor(both[:, 1, :, :], stat_o[:, :, 0, :], share[:, :, :], ALU.subtract).then_inc(merge_in, 1)
                dve.wait_ge(merge_exp, g + 1)
                nc.vector.tensor_tensor(both[:, 0, :, :], merge[:, 0, :, :], stat[:, :, 1, :], ALU.mult)
                link(nc.vector.tensor_tensor(both[:, 1, :, :], merge[:, 1, :, :], stat_o[:, :, 1, :], ALU.mult))
                link(nc.vector.tensor_tensor(share[:, :, :], both[:, 0, :, :], both[:, 1, :, :], ALU.add))
                link(nc.vector.reciprocal(share[:, :, :], share[:, :, :]))
                link(nc.vector.tensor_tensor(share[:, :, :], share[:, :, :], merge[:, 0, :, :], ALU.mult))
                for i in range(2 * ST):
                    n = P if i == 0 else 2 * P
                    ins = nc.vector.tensor_scalar(probs[:, i, 0:n], probs[:, i, 0:n],
                                                  share[:, i // ST, i % ST:i % ST + 1], None, ALU.mult)
                    if i % ST == ST - 1:
                        ins.then_inc(scaled, 1)

            def copy_even(g, b):
                dve.wait_ge(T_done, 4 * g + b + 1)
                nc.vector.tensor_copy(pT[:, BATCHES[b][0]:BATCHES[b][-1] + 1, :],
                                      p_T[0][:, 0:len(BATCHES[b]) * P].rearrange("p (a b) -> p a b", b=P))\
                    .then_inc(T_even, 1)

            def at_output(g):
                dve.wait_ge(O_done, H + g + 1)
                nc.vector.tensor_tensor(y_f[:, :], p_O[:, :], sg[:, :], ALU.mult).then_inc(y_made, 1)

            def at_body(q, last):
                links = 0

                def link(ins):
                    nonlocal links
                    links += 1
                    ins.then_inc(link_at, 1)
                    dve.wait_ge(link_at, q * LINKS_AT + links)

                bias_r_flat = bias_r[:, :, :].rearrange("p a b -> p (a b)")
                for h in range(HQ):
                    g, before = head(q, h), head(q, h - 1) if h else None
                    for i in range(7):
                        if i == K1 and h:
                            at_output(before)
                            y_low(before + H, h - 1)
                        if i == K1:
                            biases(g, 0, bias_n[:, :], nat_done, bias_loaded[0], p_S, nat_logits, link)
                        if i == GA:
                            biases(g, ST, bias_r_flat, res_done, bias_loaded[1], p_S, res_logits, link)
                        if i == K0 and h:
                            merge_and_scale(link, before)
                        split_lo(AT, q, 7 * h + i, last)
                        if i == GA:
                            gate(AT, q, h, H + g, 7 * h + GA)
                        if i == K0 and h:
                            copy_even(before, 0)
                            copy_even(before, 2)
                g = head(q, HQ - 1)
                if last:
                    for k in range(5):
                        add_out(AT, q, AT.heads + k, k)
                merge_and_scale(link, g)
                copy_even(g, 0)
                if last:
                    add_out(AT, q, AT.heads + 5, 5)
                    add_out(AT, q, AT.heads + 6, 6)
                copy_even(g, 2)
                if last:
                    add_out(AT, q, AT.heads + 7, 7)
                if not last:
                    split_lo(AT, q, AT.heads, last)
                at_output(g)
                y_low(g + H, HQ - 1)
                if not last:
                    for n in range(1, AT.pro):
                        split_lo(AT, q, AT.heads + n, last)
                out_shares(AT, q, last)
                assert links == LINKS_AT, links
            quads(dve, at_body)

            dve.wait_ge(const_loaded[0], 32)
            dve.wait_ge(fin_sq, ST)
            nc.vector.tensor_scalar(cols[:, 0:ST], cols[:, 0:ST], 1.0 / D, EPS, ALU.mult, ALU.add).then_inc(fin_base, 1)
            for t in range(ST):
                dve.wait_ge(fin_rstd, t + 1)
                for i in range(2):
                    nc.vector.scalar_tensor_tensor(out=fin[t][:, i, :], in0=final_bank(t, i)[:, :],
                                                   scalar=cols[:, 12 + t:13 + t], in1=fg_bc[:, i * S:(i + 1) * S],
                                                   op0=ALU.mult, op1=ALU.mult).then_inc(fin_ready, 1)


def bucket_of(dist):
    exact = BUCKETS // 2
    df = np.maximum(dist, 1).astype(np.float32)
    large = exact + (np.log(df / np.float32(exact)) / np.float32(np.log(2048 / exact)) * np.float32(BUCKETS - exact)).astype(np.int32)
    return np.where(dist < exact, dist, np.minimum(large, BUCKETS - 1))


def shape_constants():
    consts = np.zeros((P, 2 * P + S), np.float32)
    consts[:, 0:P] = np.eye(P)
    consts[:, P:2 * P] = np.triu(np.ones((P, P)))
    consts[:, 2 * P:] = (np.arange(S) % CH != 0)
    onehot = np.zeros((BUCKETS, GROUPS, EXT), np.float32)
    relmask = np.full((H, GROUPS, EXT), MASKED, np.float32)
    for g, (window, dilation) in enumerate(((128, 1), (512, 4), (2048, 16))):
        order = 1 if g == 0 else RES
        for e in range(EXT):
            apart = 2 * P - 1 - e
            dist = apart * order
            if apart >= 0 and dist % dilation == 0 and dist <= window:
                onehot[bucket_of(np.array(dist)), g, e] = 1.0
                relmask[:, g, e] = 0.0
    return consts, onehot.reshape(BUCKETS, -1), relmask.reshape(H, -1)


def kernel(**inputs):
    import concourse.bacc as bacc
    from concourse.bass_utils import run_bass_kernel_spmd

    nc = bacc.Bacc("TRN2", target_bir_lowering=False, num_devices=1)
    consts, onehot, relmask = shape_constants()
    a = {n: np.ascontiguousarray(v) for n, v in inputs.items()}
    arrays = {
        "x": a["x"].reshape(S, D), "ln_g": a["ln_g"], "hg_w_in": a["hg_w_in"].reshape(D, -1),
        "hg_lb": a["hg_lb_logits"], "hg_norm": a["hg_norm_g"], "hg_w_out": a["hg_w_out"].reshape(W, D),
        "at_w_in": a["att_w_in"].reshape(D, -1), "at_w_out": a["att_w_out"].reshape(W, D),
        "rel_bias": a["rel_bias"], "final_g": a["final_g"], "consts": consts, "onehot": onehot, "relmask": relmask,
    }
    args = [nc.dram_tensor(n, v.shape, F32, kind="ExternalInput").ap() for n, v in arrays.items()]
    out = nc.dram_tensor("out", (S, D), F32, kind="ExternalOutput").ap()
    program(nc, *args, out)
    result = run_bass_kernel_spmd(nc, [arrays], core_ids=[0])
    return result.results[0]["out"].reshape(1, S, D)
```

```python
from contextlib import ExitStack

import numpy as np

import concourse.bass as bass
from concourse import mybir

F32 = mybir.dt.float32
F32R = mybir.dt.float32r
ALU = mybir.AluOpType
ACT = mybir.ActivationFunctionType
AX = mybir.AxisListType
ds = bass.ds

P = 128
S = 512
D = 1024
W = 2048
KT = D // P
H = W // P
HQ = 4
NQ = H // HQ
ST = S // P
CH = 32
NC = P // CH
GROUPS = 3
RES = 4
BUCKETS = 32
EPS = 1e-6
QSCALE = float(P) ** -0.5
MASKED = -1e30
LN_MAX = 2.0 ** 63
SLOTS = 4
TW = 1024
BANKS = 3
EXT = 384


class Layer:

    def __init__(self, tile0, event0, value0, per_head, groups):
        self.value0 = value0
        self.per_head, self.groups = per_head, groups
        self.tile0, self.event0 = tile0, event0
        self.pro = 4 * groups
        self.heads = HQ * per_head
        self.T = self.heads + self.pro + 4
        self.EV = self.heads + self.pro + 8
        assert self.T % SLOTS == 0 and self.EV % BANKS == 0 and tile0 % SLOTS == 0
        self.tiles = self.pro + (NQ - 1) * self.T + self.heads + 4
        self.events = self.pro + (NQ - 1) * self.EV + self.heads + 16

    def tile(self, q, n):
        first = self.tile0 + n + (0 if q is None else self.pro)
        off = 0 if q is None else q * self.T
        turn = 0 if q is None else q * (self.T // SLOTS)
        return off + first, first % SLOTS, turn + first // SLOTS

    def event(self, q, n):
        first = self.event0 + n + (0 if q is None else self.pro)
        off = 0 if q is None else q * self.EV
        turn = 0 if q is None else q * (self.EV // BANKS)
        return off + first, first % BANKS, turn + first // BANKS

    def kind(self, n, last):
        if n < self.heads:
            return "head", n // self.per_head, n % self.per_head
        n -= self.heads
        if not last:
            if n < self.pro:
                return "value", n // 4, n % 4
            n -= self.pro
        return "out", 0, n

    def quad_tiles(self, last):
        return self.heads + 4 + (0 if last else self.pro)


HG = Layer(0, 0, 0, 3, 1)
AT = Layer(HG.tiles, HG.events, 3 * NQ * HG.groups, 7, GROUPS)
HG_COLS = (1 * W, 0 * W, 3 * W)
AT_COLS = (0, W, 3 * W, 4 * W, 6 * W, 7 * W, 9 * W)
HG_VALUE = (2 * W,)
AT_VALUE = (2 * W, 5 * W, 8 * W)
F_, Q_, G_ = 0, 1, 2
Q0, K0, Q1, K1, Q2, K2, GA = range(7)
LINKS_HG = 4 * 11
LINKS_AT = 4 * 7
TILES = [(0, 0)] + [(b, c) for b in range(1, ST) for c in (b - 1, b)] + [(r, g) for r in range(RES) for g in (1, 2)]
NATURAL = 2 * ST - 1
BATCHES = [range(i, min(i + 4, len(TILES))) for i in range(0, len(TILES), 4)]


def program(nc, x, ln_g, hg_w_in, hg_lb, hg_norm, hg_w_out, at_w_in, at_w_out, rel_bias, final_g,
            consts, onehot, relmask, out):
    ctx = ExitStack()
    with ctx:
        def sb(name, shape, dt=F32):
            return ctx.enter_context(nc.sbuf_tensor(name, shape, dt))

        def sem(name):
            return ctx.enter_context(nc.semaphore(name))

        x_v = x.rearrange("(t p) d -> t p d", p=P)
        out_v = out.rearrange("(t p) d -> t p d", p=P)
        w_in = {HG: hg_w_in.rearrange("(k p) n -> p k n", p=P), AT: at_w_in.rearrange("(k p) n -> p k n", p=P)}
        w_out = {HG: hg_w_out.rearrange("(k p) n -> p k n", p=P), AT: at_w_out.rearrange("(k p) n -> p k n", p=P)}
        ext_dram = nc.dram_tensor("ext_rows", [GROUPS, H, EXT], F32, kind="Internal").ap()
        bias_dram = nc.dram_tensor("bias_tiles", [H, P, 4 * P], F32, kind="Internal").ap()
        nat_dram = nc.dram_tensor("natural_stats", [2, S], F32, kind="Internal").ap()
        res_dram = nc.dram_tensor("residue_stats", [2, S], F32, kind="Internal").ap()

        ident = sb("ident", [P, P])
        causal = sb("causal", [P, P])
        restart = sb("restart", [P, S])
        ones = sb("ones", [P, P])
        ones_r = sb("ones_r", [P, P], F32R)
        param = sb("param", [P, 80])
        lb = sb("lb", [P, H])
        oml = sb("oml", [P, H])
        eps = sb("eps", [P, 1])
        u = {"hi": sb("u_hi", [P, KT, S], F32R), "lo": sb("u_lo", [P, KT, S], F32R)}
        hT = sb("hT", [P, KT, S])
        raw = sb("raw", [P, SLOTS, TW])
        w = {"hi": sb("w_hi", [P, SLOTS, TW], F32R), "lo": sb("w_lo", [P, SLOTS, TW], F32R)}
        y = {"hi": sb("y_hi", [P, HQ, S], F32R), "lo": sb("y_lo", [P, HQ, S], F32R)}
        v_sb = [sb(f"v{g}", [P, ST, S]) for g in range(GROUPS)]
        y_f = sb("y_f", [P, S])
        eg = sb("eg", [P, S])
        sg = sb("sg", [P, S])
        tmp = sb("tmp", [P, 2, S])
        osq_hi, osq_lo = sb("osq_hi", [P, S], F32R), sb("osq_lo", [P, S], F32R)
        osq = {"hi": osq_hi[:, :], "lo": osq_lo[:, :]}
        rstd = sb("rstd", [P, S])
        rows = sb("rows", [P, 10, S])
        ef, fg, kk, lnf, bb, eb, enb, qd, qs, sT = [rows[:, i, :] for i in range(10)]
        keys = sb("keys", [P, ST, NC + 1, P])
        dec = sb("dec", [P, ST, NC + 1])
        kT = sb("kT", [P, ST - 1, P])
        state = sb("state", [P, ST - 1, P])
        qk = sb("qk", [P, 6, S])
        flat_rows = rows[:, :, :].rearrange("p a b -> p (a b)")
        pT = flat_rows[:, 0:len(TILES) * P].rearrange("p (a b) -> p a b", b=P)
        probs = flat_rows[:, 4 * S:8 * S].rearrange("p (a b) -> p a b", b=2 * P)
        bias_n = sb("bias_n", [P, 2 * P])
        bias_r = sb("bias_r", [P, 2, P])
        stat = sb("stat", [P, 2, 2, ST])
        stat_o = sb("stat_o", [P, 2, 2, ST])
        negm = sb("negm", [P, 2 * ST])
        both = sb("both", [P, 2, 2, ST])
        merge = sb("merge", [P, 2, 2, ST])
        share = sb("share", [P, 2, ST])
        cols = sb("cols", [P, 16])
        nat = [v_sb[1 + t // 2][:, 2 * (t % 2):2 * (t % 2) + 2, :] for t in range(ST)]
        spare = [qk[:, 0:2, :], qk[:, 2:4, :], qk[:, 4:6, :], rows[:, 8:10, :]]
        prow = probs[:, :, :].rearrange("p a b -> p (a b)")
        onehot_sb = pT[:, :, :].rearrange("p a b -> p (a b)")[0:BUCKETS, 0:GROUPS * EXT]
        relmask_sb = keys[:, :, :, :].rearrange("p a b c -> p (a b c)")[0:H, 0:GROUPS * EXT]
        ext_sb = keys[:, :, :, :].rearrange("p a b c -> p (a b c)")[0:H, GROUPS * EXT:2 * GROUPS * EXT]
        relb_sb = bias_n[0:BUCKETS, 0:GROUPS * H]
        fg_bc = v_sb[0][:, 0:2, :].rearrange("p a b -> p (a b)")

        proj = [ctx.enter_context(nc.psum_tensor(f"proj{i}", [P, S], F32)) for i in range(BANKS)]
        inner = [ctx.enter_context(nc.psum_tensor(f"inner{i}", [P, S], F32)) for i in range(5)]
        p_sc, p_kT, p_U, p_O, p_ss = inner
        p_S = inner[0:2]
        p_T = (inner[2], inner[4])

        x_loaded = [sem(f"x_loaded{i}") for i in range(ST)]
        const_loaded = [sem(f"const_loaded{i}") for i in range(8)]
        loaded = [sem(f"loaded{i}") for i in range(SLOTS)]
        bank_free = [sem(f"bank_free{i}") for i in range(BANKS)]

        def sems(names):
            return [sem(n) for n in names.split()]

        ones_ready, ones_r_ready, eps_ready, x_T, x_copied = sems("ones_ready ones_r_ready eps_ready x_T x_copied")
        x_squared, x_rstd_step, x_rstd, diag_ready, rstd_spread = sems("x_squared x_rstd_step x_rstd diag_ready rstd_spread")
        param_T, param_ready, lb_step, lb_exp = sems("param_T param_ready lb_step lb_exp")
        ext_done, ext_ready, ext_stored, bias_stored = sems("ext_done ext_ready ext_stored bias_stored")
        sp_met, pool_met = sems("sp_met pool_met")
        hi_ready, w_ready, value_tile_done, proj_done = sems("hi_ready w_ready value_tile_done proj_done")
        sq_ready, ss_done, rstd_step = sems("sq_ready ss_done rstd_step")
        rstd_ready, u_made, u_hi_ready, u_ready = sems("rstd_ready u_made u_hi_ready u_ready")
        link_hg, link_at = sems("link_hg link_at")
        sigf_bounded, sigf_step, sigf_ready = sems("sigf_bounded sigf_step sigf_ready")
        sigma_bounded, sigma_step, sigma_ready = sems("sigma_bounded sigma_step sigma_ready")
        f_ready, lnf_ready, b_ready, eb_ready = sems("f_ready lnf_ready b_ready eb_ready")
        q_ready, keys_ready, scores_done, sT_ready = sems("q_ready keys_ready scores_done sT_ready")
        kT_done, kT_ready, U_done, state_ready = sems("kT_done kT_ready U_done state_ready")
        squared, osq_hi_ready, osq_ready = sems("squared osq_hi_ready osq_ready")
        osum_done, orstd_step, orstd_ready = sems("osum_done orstd_step orstd_ready")
        O_done, y_made, y_hi_ready, y_ready = sems("O_done y_made y_hi_ready y_ready")
        nat_done, res_done, nat_logits = sems("nat_done res_done nat_logits")
        res_logits, nat_probs, res_probs, bias_used = sems("res_logits nat_probs res_probs bias_used")
        stat_a, stat_b, merge_in, merge_exp = sems("stat_a stat_b merge_in merge_exp")
        scaled, T_done, T_even, T_odd = sems("scaled T_done T_even T_odd")
        fin_T, fin_base, fin_sq, fin_step, fin_rstd, fin_ready = sems("fin_T fin_base fin_sq fin_step fin_rstd fin_ready")
        bias_loaded = [sem("bias_n_loaded"), sem("bias_r_loaded")]
        out_stored = [sem(f"out_stored{i}") for i in range(2 * ST)]

        def head(q, h):
            return q * HQ + h

        def quads(eng, body):
            with eng.Fori(0, NQ - 1) as q:
                body(q, False)
            body(NQ - 1, True)

        def wait_turn(eng, met, signal, value):
            eng.wait_ge(signal, value)
            eng.sem_inc(met, 1)

        def wait_emptied(eng, layer, q, e):
            _, bank, before = layer.event(q, e)
            eng.wait_ge(bank_free[bank], before + 1)

        def wait_tile_done(eng, layer, q, n, last):
            if q is None:
                kind, group, part = "value", n // 4, n % 4
                count, e = layer.value0 + 3 * group + part + 1, 4 * group + 3
            else:
                kind, group, part = layer.kind(n, last)
                count = layer.value0 + 3 * layer.groups * (q + 1) + 3 * group + part + 1
                e = {"head": n, "value": layer.heads + 4 * group + 3,
                     "out": layer.heads + (8 if last else layer.pro) + 2 * part + 1}[kind]
            if kind == "value" and part < 3:
                eng.wait_ge(value_tile_done, count)
            else:
                eng.wait_ge(proj_done, layer.event(q, e)[0] + 1)

        def value_bank(layer, q, e):
            first = 0 if q is None else layer.heads
            if (layer is AT or q is None) and e == first + ST - 1:
                return inner[0]
            return proj[layer.event(q, e)[1]]

        def final_bank(t, half):
            return inner[t] if half == 0 else inner[ST] if t == 0 else proj[t - 1]

        FIRST_HALVES = ST * KT // 2
        def second_half(t):
            return FIRST_HALVES + (t + 1) * KT // 2

        block = ctx.enter_context(nc.Block())

        @block.sync
        def _(sp):
            def tile_source(layer, q, kind, group, part):
                if kind == "head":
                    cols = (HG_COLS if layer is HG else AT_COLS)[part]
                    return w_in[layer][:, :, ds(head(q, group) * P + cols, P)], KT
                if kind == "value":
                    col = (HG_VALUE if layer is HG else AT_VALUE)[group]
                    return w_in[layer][:, 2 * part:2 * part + 2, ds(q * (HQ * P) + col, HQ * P)], 2
                return w_out[layer][:, ds(q * HQ, HQ), part * 2 * P:(part + 1) * 2 * P], HQ

            def load(slot, source, k):
                sp.dma_start(raw[:, slot, :].rearrange("p (k n) -> p k n", k=k), source).then_inc(loaded[slot], 16)

            def load_after(layer, q, n, last):
                number, slot, _ = layer.tile(q, n)
                ahead = n + SLOTS
                if q is None:
                    where = (None, "value", ahead // 4, ahead % 4) if ahead < layer.pro else \
                        (0, *layer.kind(ahead - layer.pro, False))
                elif ahead < layer.quad_tiles(last):
                    what = layer.kind(ahead, last)
                    where = (q + 1 if what[0] == "value" else q, *what)
                elif not last:
                    where = (q + 1, *layer.kind(ahead - layer.T, False))
                elif layer is HG:
                    where, layer = (None, "value", 0, ahead - layer.quad_tiles(last)), AT
                else:
                    return
                wait_turn(sp, sp_met, w_ready, number + 1)
                load(slot, *tile_source(layer, 0 if where[0] is None else where[0], *where[1:]))

            def load_x(t):
                sp.dma_start(nat[t].rearrange("p a b -> p (a b)"), x_v[t]).then_inc(x_loaded[t], 16)

            load_x(0)
            sp.dma_start(ident[:, :], consts[:, 0:P]).then_inc(const_loaded[0], 16)
            for t in range(1, ST):
                load_x(t)
            sp.dma_start(prow[0:48, 0:P], hg_lb.rearrange("r (h p) -> (r h) p", p=P)).then_inc(const_loaded[1], 16)
            sp.dma_start(prow[48:64, 0:P], hg_norm.rearrange("r (h p) -> (r h) p", p=P)).then_inc(const_loaded[2], 16)
            sp.dma_start(prow[64:80, 0:P], ln_g.rearrange("r (h p) -> (r h) p", p=P)).then_inc(const_loaded[3], 16)
            for n in range(SLOTS):
                load(n, *tile_source(HG, 0, "value", 0, n))
            sp.dma_start(causal[:, :], consts[:, P:2 * P]).then_inc(const_loaded[4], 16)
            sp.dma_start(restart[:, :], consts[:, 2 * P:2 * P + S]).then_inc(const_loaded[4], 16)
            sp.dma_start(onehot_sb, onehot).then_inc(const_loaded[5], 16)
            sp.dma_start(relmask_sb, relmask).then_inc(const_loaded[6], 16)
            sp.dma_start(relb_sb, rel_bias).then_inc(const_loaded[7], 16)
            for layer in (HG, AT):
                for n in range(layer.pro):
                    load_after(layer, None, n, False)
                if layer is HG:
                    sp.wait_ge(ext_ready, GROUPS)
                    sp.dma_start(ext_dram.rearrange("g h e -> h g e"),
                                 ext_sb.rearrange("h (g e) -> h g e", g=GROUPS)).then_inc(ext_stored, 16)

                def body(q, last):
                    for n in range(layer.quad_tiles(last)):
                        load_after(layer, q, n, last)
                quads(sp, body)
            sp.wait_ge(O_done, 2 * H)
            sp.dma_start(fg_bc, final_g.rearrange("(a d) -> a d", a=1).broadcast_to([P, D])).then_inc(const_loaded[0], 16)
            for i in range(2 * ST):
                sp.wait_ge(fin_ready, i + 1)
                sp.dma_start(out_v[i // 2, :, (i % 2) * S:(i % 2 + 1) * S], nat[i // 2][:, i % 2, :])\
                    .then_inc(out_stored[i], 16)
            for s in out_stored:
                sp.wait_ge(s, 16)
            sp.wait_ge(ext_stored, 16)

        @block.gpsimd
        def _(pool):
            nc.gpsimd.memset(ones[:, :], 1.0).then_inc(ones_ready, 1)
            def load_bias(g):
                pool.dma_start(bias_n[:, :], bias_dram[ds(g, 1), :, 0:2 * P].rearrange("a p n -> p (a n)"))\
                    .then_inc(bias_loaded[0], 16)
                pool.dma_start(bias_r[:, :, :], bias_dram[ds(g, 1), :, 2 * P:].rearrange("a p (k n) -> p (a k) n", k=2))\
                    .then_inc(bias_loaded[1], 16)

            pool.wait_ge(ext_stored, 16)
            for g, first, n in ((0, P - 1, 2 * P), (1, 2 * P - 1, P), (2, 2 * P - 1, P)):
                to = (0, 2 * P, 3 * P)[g]
                pool.dma_start(bias_dram[:, :, to:to + n],
                               bass.AP(ext_dram.tensor, g * H * EXT + first, [[EXT, H], [-1, P], [1, n]]))\
                    .then_inc(bias_stored, 16)
            pool.wait_ge(bias_stored, 16 * GROUPS)
            load_bias(0)

            def body(q, last):
                for h in range(HQ):
                    g = head(q, h)
                    if not (last and h == HQ - 1):
                        wait_turn(pool, pool_met, bias_used, 2 * g + 2)
                        load_bias(g + 1)
            quads(pool, body)

        @block.tensor
        def _(pe):
            def split_matmuls(bank, stationary, moving, first, last):
                ins = None
                for n, (a, b) in enumerate((("hi", "hi"), ("hi", "lo"), ("lo", "hi"))):
                    ins = nc.tensor.matmul(bank[:, :], stationary(a), moving(b),
                                           start=(first and n == 0), stop=(last and n == 2))
                return ins

            def head_tile(layer, q, n, half):
                number, slot, _ = layer.tile(q, n)
                _, bank, before = layer.event(q, n)
                if half == 0:
                    pe.wait_ge(w_ready, number + 1)
                    pe.wait_ge(bank_free[bank], before)
                for k in range(half * KT // 2, (half + 1) * KT // 2):
                    ins = split_matmuls(proj[bank], lambda a: w[a][:, slot, k * P:(k + 1) * P],
                                        lambda b: u[b][:, k, :], k == 0, k == KT - 1)
                if half:
                    ins.then_inc(proj_done, 1)

            def values(layer, q, group, s, half):
                first = 4 * group + (0 if q is None else layer.heads)
                _, bank, before = layer.event(q, first + s)
                psum = value_bank(layer, q, first + s)
                if half == 0 and psum is proj[bank]:
                    pe.wait_ge(bank_free[bank], before)
                for i in range(2 * half, 2 * half + 2):
                    number, slot, _ = layer.tile(q, first + i)
                    if s == 0:
                        pe.wait_ge(w_ready, number + 1)
                    for k in (2 * i, 2 * i + 1):
                        cols = slice(s, S, RES) if group else slice(s * P, (s + 1) * P)
                        ins = split_matmuls(psum, lambda a: u[a][:, k, cols],
                                            lambda b: w[b][:, slot, (k % 2) * S:(k % 2 + 1) * S], k == 0, k == KT - 1)
                    if i == 3:
                        ins.then_inc(proj_done, 1)
                    elif s == ST - 1:
                        ins.then_inc(value_tile_done, 1)

            def first_values(layer, u_before):
                for k in range(KT):
                    if layer is HG and k == KT // 2:
                        bias_rows()
                    number, slot, _ = layer.tile(None, k // 2)
                    if k % 2 == 0:
                        pe.wait_ge(w_ready, number + 1)
                    pe.wait_ge(u_ready, u_before + k + 1)
                    for s in range(ST):
                        _, bank, before = layer.event(None, s)
                        if k == 0 and layer is AT and s < BANKS:
                            pe.wait_ge(bank_free[bank], before)
                        ins = split_matmuls(value_bank(layer, None, s), lambda a: u[a][:, k, s * P:(s + 1) * P],
                                            lambda b: w[b][:, slot, (k % 2) * S:(k % 2 + 1) * S], k == 0, k == KT - 1)
                        if k == KT - 1:
                            ins.then_inc(proj_done, 1)
                        elif k % 2 and s == ST - 1:
                            ins.then_inc(value_tile_done, 1)

            def bias_rows():
                pe.wait_ge(const_loaded[5], 16)
                pe.wait_ge(const_loaded[7], 16)
                for g in range(GROUPS):
                    nc.tensor.matmul(inner[1 + g][0:H, 0:EXT], relb_sb[:, g * H:(g + 1) * H],
                                     onehot_sb[:, g * EXT:(g + 1) * EXT], start=True, stop=True).then_inc(ext_done, 1)

            def out_column(layer, q, tile, event, c, heads):
                number, slot, _ = layer.tile(q, tile)
                _, bank, before = layer.event(q, event)
                pe.wait_ge(w_ready, number + 1)
                pe.wait_ge(bank_free[bank], before)
                for k in heads:
                    if c == 0:
                        pe.wait_ge(y_ready, (0 if layer is HG else H) + head(q, k) + 1)
                    at = (2 * k + c % 2) * P
                    ins = split_matmuls(proj[bank], lambda a: w[a][:, slot, at:at + P],
                                        lambda b: y[b][:, k, :], k == heads[0], k == heads[-1])
                ins.then_inc(proj_done, 1)

            def final_transposes(k):
                wait_emptied(pe, AT, NQ - 1, AT.heads + KT + k)
                for t in range(ST if k < KT // 2 else 1):
                    final_transpose(t, k)
                if k == KT - 1:
                    for t in range(1, ST):
                        for kk in range(KT // 2, KT):
                            final_transpose(t, kk)

            def final_transpose(t, k):
                nc.tensor.transpose(final_bank(t, k // 4)[:, (k % 4) * P:(k % 4 + 1) * P],
                                    hT[:, k, t * P:(t + 1) * P], ident[:, :]).then_inc(fin_T, 1)

            def out_projection(layer, q, last):
                tile = layer.heads + (0 if last else layer.pro)
                for c in range(KT):
                    out_column(layer, q, tile + c // 2, tile + c + (KT if last else 0), c, (HQ - 1,) if last else range(HQ))
                    if last and c >= 2:
                        (sum_squares if layer is HG else final_transposes)(c - 2)

            def sum_squares(k):
                pe.wait_ge(sq_ready, k + 1)
                nc.tensor.matmul(p_ss[:, :], ones[:, :], tmp[:, k % 2, :],
                                 start=(k == 0), stop=(k == KT - 1)).then_inc(ss_done, 1)

            pe.wait_ge(ones_ready, 1)
            pe.wait_ge(const_loaded[0], 16)
            for i in range(ST * KT):
                t, k = i // KT, i % KT
                if k == 0:
                    pe.wait_ge(x_loaded[t], 16)
                if i >= 16 and i % 4 == 0:
                    pe.wait_ge(x_copied, i // 4 - 3)
                nc.tensor.transpose(inner[(i // 4) % 4][:, (i % 4) * P:(i % 4 + 1) * P],
                                    nat[t][:, k // 4, (k % 4) * P:(k % 4 + 1) * P], ident[:, :]).then_inc(x_T, 1)
            for i in (1, 2, 3):
                pe.wait_ge(const_loaded[i], 16)
            nc.tensor.transpose(proj[0][:, 0:80], prow[0:80, 0:P], ident[0:80, 0:80]).then_inc(param_T, 1)
            pe.wait_ge(diag_ready, 1)
            nc.tensor.matmul(p_ss[:, :], ones[:, :], y_f[:, :], start=True, stop=True).then_inc(rstd_spread, 1)

            pe.wait_ge(param_ready, 1)
            first_values(HG, 0)
            pe.wait_ge(ones_r_ready, 1)
            def scores(g):
                pe.wait_ge(keys_ready, g + 1)
                for b in range(ST):
                    for j in range(NC):
                        seen = (j + 1) * CH
                        ins = nc.tensor.matmul(p_sc[0:seen, b * P + j * CH:b * P + (j + 1) * CH], keys[:, b, j, 0:seen],
                                               qd[:, b * P + j * CH:b * P + (j + 1) * CH], start=True, stop=True)
                ins.then_inc(scores_done, 1)
                for b in range(ST - 1):
                    ins = nc.tensor.transpose(p_kT[:, b * P:(b + 1) * P], keys[:, b, NC, :], ident[:, :])
                ins.then_inc(kT_done, 1)

            def updates(g, h):
                pe.wait_ge(kT_ready, g + 1)
                for b in range(ST - 1):
                    ins = nc.tensor.matmul(p_U[:, b * P:(b + 1) * P], kT[:, b, :], v_sb[0][:, b, h * P:(h + 1) * P],
                                           start=True, stop=True)
                ins.then_inc(U_done, 1)

            def outputs(g, h):
                pe.wait_ge(q_ready, g + 1)
                pe.wait_ge(sT_ready, g + 1)
                pe.wait_ge(state_ready, g + 1)
                for b in range(ST):
                    s = slice(b * P, (b + 1) * P)
                    ins = nc.tensor.matmul(p_O[:, s], v_sb[0][:, b, h * P:(h + 1) * P], sT[:, s],
                                           start=True, stop=(b == 0))
                    if b:
                        ins = nc.tensor.matmul(p_O[:, s], state[:, b - 1, :], qs[:, s], start=False, stop=True)
                ins.then_inc(O_done, 1)

            def norm_sum(g):
                pe.wait_ge(osq_ready, g + 1)
                nc.tensor.matmul(p_ss[:, :], ones_r[:, :], osq["hi"], start=True, stop=False)
                nc.tensor.matmul(p_ss[:, :], ones_r[:, :], osq["lo"], start=False, stop=True).then_inc(osum_done, 1)

            def recurrence(g, h, half):
                if half == 0:
                    scores(g)
                elif half == 1:
                    updates(g, h)
                elif half == 2:
                    outputs(g, h)
                elif half == 3:
                    norm_sum(g)

            def hg_body(q, last):
                for h in range(HQ):
                    for half in range(2 * HG.per_head):
                        head_tile(HG, q, HG.per_head * h + half // 2, half % 2)
                        if h:
                            recurrence(head(q, h - 1), h - 1, half)
                for half in range(KT):
                    if last:
                        out_column(HG, q, HG.heads + half // 2, HG.heads + half, half, range(HQ - 1))
                    else:
                        values(HG, q, 0, half // 2, half % 2)
                    recurrence(head(q, HQ - 1), HQ - 1, half)
                out_projection(HG, q, last)
            quads(pe, hg_body)

            sum_squares(KT - 2)
            sum_squares(KT - 1)
            first_values(AT, KT)
            for g in range(1, GROUPS):
                for s in range(ST):
                    for half in range(2):
                        values(AT, None, g, s, half)

            def natural_logits(q, h):
                wait_emptied(pe, AT, q, 7 * h + K0)
                for b in range(ST):
                    lo = max(b - 1, 0) * P
                    n = (b + 1) * P - lo
                    bank = p_S[b // 2]
                    at = (b % 2) * 2 * P
                    ins = nc.tensor.matmul(bank[:, at:at + n], qk[:, 0, b * P:(b + 1) * P], qk[:, 1, lo:lo + n],
                                           start=True, stop=True)
                    if b % 2:
                        ins.then_inc(nat_done, 1)

            def residue_logits(g, q, h):
                wait_emptied(pe, AT, q, 7 * h + K2)
                pe.wait_ge(nat_logits, g + 1)
                for r in range(RES):
                    for i in range(2):
                        s = slice(r * P, (r + 1) * P)
                        ins = nc.tensor.matmul(p_S[r // 2][:, ((r % 2) * 2 + i) * P:((r % 2) * 2 + i + 1) * P],
                                               qk[:, 2 + 2 * i, s], qk[:, 3 + 2 * i, s], start=True, stop=True)
                    if r % 2:
                        ins.then_inc(res_done, 1)

            def transposes(g, batches):
                for n in batches:
                    if n < 2:
                        pe.wait_ge(scaled, 2 * g + n + 1)
                    if n == 2:
                        pe.wait_ge(T_even, 2 * g + 1)
                    if n == 3:
                        pe.wait_ge(T_odd, 2 * g + 1)
                    for i in BATCHES[n]:
                        b, c = TILES[i]
                        if i < NATURAL:
                            src = probs[:, b, (c - b + 1 if b else 0) * P:(c - b + 2 if b else 1) * P]
                        else:
                            src = probs[:, ST + b, (c - 1) * P:c * P]
                        ins = nc.tensor.transpose(p_T[n % 2][:, (i % 4) * P:(i % 4 + 1) * P], src, ident[:, :])
                    ins.then_inc(T_done, 1)

            def attend(g, h):
                pe.wait_ge(T_even, 2 * g + 2)
                pe.wait_ge(T_odd, 2 * g + 2)
                for i, (b, c) in enumerate(TILES):
                    if i < NATURAL:
                        vals, o = v_sb[0][:, c, h * P:(h + 1) * P], p_O[:, b * P:(b + 1) * P]
                    else:
                        vals, o = v_sb[c][:, b, h * P:(h + 1) * P], p_O[:, b::RES]
                    ins = nc.tensor.matmul(o, vals, pT[:, i, :], start=(i == 0), stop=(i == len(TILES) - 1),
                                           skip_group_check=True)
                ins.then_inc(O_done, 1)

            def attention(g, h, half):
                if half == 3:
                    transposes(g, (0, 1))
                elif half == 4:
                    transposes(g, (2, 3))
                elif half == 5:
                    attend(g, h)

            def at_body(q, last):
                for h in range(HQ):
                    for half in range(2 * AT.per_head):
                        head_tile(AT, q, AT.per_head * h + half // 2, half % 2)
                        if h:
                            attention(head(q, h - 1), h - 1, half - 1)
                        if half == 2 * K1:
                            natural_logits(q, h)
                        elif half == 2 * GA:
                            residue_logits(head(q, h), q, h)
                for half in range(KT if last else 2 * AT.pro):
                    if last:
                        out_column(AT, q, AT.heads + half // 2, AT.heads + half, half, range(HQ - 1))
                        attention(head(q, HQ - 1), HQ - 1, half - 1)
                    else:
                        if half == 2 * (ST - 1):
                            pe.wait_ge(res_logits, head(q, HQ - 1) + 1)
                        values(AT, q, half // 8, half // 2 % 4, half % 2)
                        attention(head(q, HQ - 1), HQ - 1, half - 1)
                out_projection(AT, q, last)
            quads(pe, at_body)

            final_transposes(KT - 2)
            final_transposes(KT - 1)

        @block.scalar
        def _(act):
            def split_hi(layer, q, n, last):
                number, slot, use = layer.tile(q, n)
                if layer is AT and last and n + SLOTS >= layer.quad_tiles(True):
                    return
                act.wait_ge(loaded[slot], use * 16 + 32)
                wait_tile_done(act, layer, q, n, last)
                nc.scalar.activation(w["hi"][:, slot, :], raw[:, slot, :], ACT.Copy).then_inc(hi_ready, 1)

            def copy_values(layer, q, group, e):
                _, bank, _ = layer.event(q, e)
                number = layer.event(q, e)[0]
                act.wait_ge(proj_done, number + 1)
                nc.scalar.activation(v_sb[group][:, (e - (0 if q is None else layer.heads)) % ST, :],
                                     value_bank(layer, q, e)[:, :], ACT.Copy).then_inc(bank_free[bank], 1)

            def u_high(which, k):
                act.wait_ge(u_made, which * KT + k + 1)
                nc.scalar.activation(u["hi"][:, k, :], tmp[:, k % 2, :], ACT.Copy).then_inc(u_hi_ready, 1)

            def square_column(k):
                wait_emptied(act, HG, NQ - 1, HG.heads + KT + k)
                if k >= 2:
                    act.wait_ge(ss_done, k - 1)
                nc.scalar.activation(tmp[:, k % 2, :], hT[:, k, :], ACT.Square).then_inc(sq_ready, 1)

            def first_hi(n):
                act.wait_ge(loaded[n], 16)
                nc.scalar.activation(w["hi"][:, n, :], raw[:, n, :], ACT.Copy).then_inc(hi_ready, 1)

            nc.scalar.preload_act_table_set("natural_log_exp_and_others")
            for t in range(ST):
                act.wait_ge(x_loaded[t], 16)
                nc.scalar.activation(spare[t], nat[t], ACT.Square, accum_out=cols[:, t:t + 1]).then_inc(x_squared, 1)
            act.wait_ge(eps_ready, 1)
            act.wait_ge(x_squared, ST)
            nc.scalar.activation(cols[:, 4:8], cols[:, 0:4], ACT.Ln, scale=1.0 / D, bias=eps[:, :]).then_inc(x_rstd_step, 1)
            act.wait_ge(x_rstd_step, 1)
            nc.scalar.activation(cols[:, 8:12], cols[:, 4:8], ACT.Exp, scale=-0.5).then_inc(x_rstd, 1)
            first_hi(0)
            act.wait_ge(rstd_spread, 1)
            nc.scalar.activation(rstd[:, :], p_ss[:, :], ACT.Copy).then_inc(rstd_ready, 1)
            for k in range(KT):
                u_high(0, k)
                if k % 2 and k < KT - 1:
                    first_hi(k // 2 + 1)
            act.wait_ge(lb_step, 3)
            nc.scalar.activation(param[:, 0:3 * H], param[:, 0:3 * H], ACT.Exp).then_inc(lb_exp, 1)

            def first_value_events(layer):
                for i in range(3):
                    split_hi(layer, None, i, False)
                for s in range(ST):
                    copy_values(layer, None, 0, s)
                split_hi(layer, None, 3, False)

            def value_events(layer, q, group, first):
                base = 4 * group + (0 if q is None else layer.heads)
                for s in range(first, ST):
                    if s == ST - 1:
                        for i in range(3):
                            split_hi(layer, q, base + i, False)
                    copy_values(layer, q, group, base + s)
                split_hi(layer, q, base + 3, False)

            act.wait_ge(ones_ready, 1)
            nc.scalar.activation(ones_r[:, :], ones[:, :], ACT.Copy).then_inc(ones_r_ready, 1)
            first_value_events(HG)

            def kT_copy(g):
                act.wait_ge(kT_done, g + 1)
                nc.scalar.activation(kT[:, :, :].rearrange("p a b -> p (a b)"), p_kT[:, 0:(ST - 1) * P], ACT.Copy)\
                    .then_inc(kT_ready, 1)

            def square(g):
                act.wait_ge(O_done, g + 1)
                nc.scalar.activation(enb[:, :], p_O[:, :], ACT.Square).then_inc(squared, 1)
                act.wait_ge(squared, g + 1)
                nc.scalar.activation(osq["hi"], enb[:, :], ACT.Copy).then_inc(osq_hi_ready, 1)

            def out_rstd(g):
                act.wait_ge(osum_done, g + 1)
                nc.scalar.activation(rstd[:, :], p_ss[:, :], ACT.Ln, scale=1.0 / P, bias=eps[:, :]).then_inc(orstd_step, 1)
                act.wait_ge(orstd_step, g + 1)
                nc.scalar.activation(rstd[:, :], rstd[:, :], ACT.Exp, scale=-0.5).then_inc(orstd_ready, 1)

            def y_high(g, slot):
                act.wait_ge(y_made, g + 1)
                nc.scalar.activation(y["hi"][:, slot, :], y_f[:, :], ACT.Copy).then_inc(y_hi_ready, 1)

            def sigmoid(g):
                act.wait_ge(sigma_bounded, g + 1)
                nc.scalar.activation(eg[:, :], eg[:, :], ACT.Ln, bias=ones[:, 0:1]).then_inc(sigma_step, 1)
                act.wait_ge(sigma_step, 2 * g + 2)
                nc.scalar.activation(eg[:, :], eg[:, :], ACT.Exp, scale=-1.0).then_inc(sigma_ready, 1)

            def hg_body(q, last):
                for h in range(HQ):
                    g, before = head(q, h), head(q, h - 1) if h else None
                    number, bank, _ = HG.event(q, 3 * h + F_)
                    if h:
                        kT_copy(before)
                    act.wait_ge(proj_done, number + 1)
                    nc.scalar.activation(ef[:, :], proj[bank][:, :], ACT.Exp, scale=-1.0).then_inc(bank_free[bank], 1)
                    act.wait_ge(sigf_bounded, g + 1)
                    nc.scalar.activation(ef[:, :], ef[:, :], ACT.Ln, bias=ones[:, 0:1]).then_inc(sigf_step, 1)
                    act.wait_ge(sigf_step, g + 1)
                    nc.scalar.activation(ef[:, :], ef[:, :], ACT.Exp, scale=-1.0).then_inc(sigf_ready, 1)
                    split_hi(HG, q, 3 * h + F_, last)
                    act.wait_ge(f_ready, g + 1)
                    nc.scalar.activation(lnf[:, :], fg[:, :], ACT.Ln).then_inc(lnf_ready, 1)
                    if h:
                        square(before)
                    act.wait_ge(b_ready, g + 1)
                    nc.scalar.activation(eb[:, :], bb[:, :], ACT.Exp).then_inc(eb_ready, 1)
                    if h:
                        out_rstd(before)
                    nc.scalar.activation(enb[:, :], bb[:, :], ACT.Exp, scale=-1.0).then_inc(eb_ready, 1)
                    split_hi(HG, q, 3 * h + Q_, last)
                    if h:
                        y_high(before, h - 1)
                    number, bank, _ = HG.event(q, 3 * h + G_)
                    act.wait_ge(proj_done, number + 1)
                    nc.scalar.activation(eg[:, :], proj[bank][:, :], ACT.Exp, scale=-1.0).then_inc(sigma_step, 1)
                    split_hi(HG, q, 3 * h + G_, last)
                    sigmoid(g)
                g = head(q, HQ - 1)
                kT_copy(g)
                square(g)
                if not last:
                    copy_values(HG, q, 0, HG.heads)
                    copy_values(HG, q, 0, HG.heads + 1)
                out_rstd(g)
                y_high(g, HQ - 1)
                if not last:
                    value_events(HG, q, 0, 2)
                for i in range(4):
                    if last:
                        square_column(2 * i)
                        square_column(2 * i + 1)
                    if not last or i % 2:
                        split_hi(HG, q, HG.quad_tiles(last) - 4 + (i // 2 if last else i), last)
            quads(act, hg_body)

            act.wait_ge(ss_done, KT)
            nc.scalar.activation(rstd[:, :], p_ss[:, :], ACT.Ln, scale=1.0 / D, bias=eps[:, :]).then_inc(rstd_step, 1)
            act.wait_ge(rstd_step, 1)
            nc.scalar.activation(rstd[:, :], rstd[:, :], ACT.Exp, scale=-0.5).then_inc(rstd_ready, 1)
            for k in range(KT):
                u_high(1, k)
                if k in (1, 3):
                    split_hi(HG, NQ - 1, HG.quad_tiles(True) - 2 + k // 2, True)
            first_value_events(AT)
            for g in range(1, GROUPS):
                value_events(AT, None, g, 0)

            def exps(g, first, logits, signal):
                act.wait_ge(logits, g + 1)
                for b in range(ST):
                    i = first + b
                    n = P if i == 0 else 2 * P
                    nc.scalar.activation(probs[:, i, 0:n], probs[:, i, 0:n], ACT.Exp, bias=negm[:, i:i + 1],
                                         accum_out=stat[:, i // ST, 1, b:b + 1]).then_inc(signal, 1)

            natural = [d.rearrange("k (b p) -> p (k b)", p=P) for d in (nat_dram, res_dram)]
            residue = [d.rearrange("k (i r) -> i k r", r=RES) for d in (nat_dram, res_dram)]

            def store_natural(g):
                act.wait_ge(nat_probs, 4 * g + 4)
                act.dma_start(natural[0], stat[:, 0, :, :].rearrange("p k b -> p (k b)"),
                              allow_slow_non_contiguous=True).then_inc(stat_a, 16)

            def load_natural(g):
                act.wait_ge(stat_a, 32 * g + 16)
                act.dma_start(stat_o[:, 1, :, :], residue[0]).then_inc(stat_a, 16)

            def store_residue(g):
                act.wait_ge(res_probs, 4 * g + 4)
                act.dma_start(residue[1], stat[:, 1, :, :]).then_inc(stat_b, 16)

            def load_residue(g):
                act.wait_ge(stat_b, 32 * g + 16)
                act.dma_start(stat_o[:, 0, :, :].rearrange("p k b -> p (k b)"), natural[1],
                              allow_slow_non_contiguous=True).then_inc(stat_b, 16)

            def merge_exps(g):
                act.wait_ge(merge_in, g + 1)
                nc.scalar.activation(merge[:, :, :, :], both[:, :, :, :], ACT.Exp).then_inc(merge_exp, 1)

            def copy_odd(g):
                for n, b in enumerate((1, 3)):
                    act.wait_ge(T_done, 4 * g + b + 1)
                    nc.scalar.activation(pT[:, BATCHES[b][0]:BATCHES[b][-1] + 1, :],
                                         p_T[1][:, 0:len(BATCHES[b]) * P].rearrange("p (a b) -> p a b", b=P),
                                         ACT.Copy).then_inc(T_odd, 1)

            def at_body(q, last):
                for h in range(HQ):
                    g, before = head(q, h), head(q, h - 1) if h else None
                    for i in range(7):
                        number, bank, _ = AT.event(q, 7 * h + i)
                        if i == K0 and h:
                            merge_exps(before)
                        if i == Q1 and h:
                            copy_odd(before)
                        if i == K1 and h:
                            y_high(before + H, h - 1)
                        if i == K1:
                            exps(g, 0, nat_logits, nat_probs)
                        if i == GA:
                            load_natural(g)
                            exps(g, ST, res_logits, res_probs)
                            if not (last and h == HQ - 1):
                                split_hi(AT, q, 7 * h + i, last)
                                store_residue(g)
                        act.wait_ge(proj_done, number + 1)
                        if i == GA:
                            nc.scalar.activation(eg[:, :], proj[bank][:, :], ACT.Exp, scale=-1.0).then_inc(sigma_step, 1)
                            if last and h == HQ - 1:
                                store_residue(g)
                            sigmoid(H + g)
                            if last and h == HQ - 1:
                                split_hi(AT, q, 7 * h + i, last)
                        else:
                            o, src = qk[:, i, :], proj[bank][:, :]
                            if i >= Q1:
                                o = qk[:, i, :].rearrange("p (r i) -> p r i", r=RES)
                                src = proj[bank][:, :].rearrange("p (i r) -> p r i", r=RES)
                            nc.scalar.activation(o, src, ACT.Copy, scale=QSCALE if i in (Q0, Q1, Q2) else 1.0)\
                                .then_inc(bank_free[bank], 1)
                            split_hi(AT, q, 7 * h + i, last)
                        if i == K1:
                            store_natural(g)
                    load_residue(g)
                g = head(q, HQ - 1)
                merge_exps(g)
                copy_odd(g)
                if not last:
                    split_hi(AT, q, AT.heads, False)
                    act.wait_ge(O_done, H + g + 1)
                    copy_values(AT, q, 0, AT.heads)
                y_high(g + H, HQ - 1)
                if not last:
                    copy_values(AT, q, 0, AT.heads + 1)
                    split_hi(AT, q, AT.heads + 1, False)
                    copy_values(AT, q, 0, AT.heads + 2)
                    split_hi(AT, q, AT.heads + 2, False)
                    copy_values(AT, q, 0, AT.heads + 3)
                    split_hi(AT, q, AT.heads + 3, False)
                    for group in range(1, GROUPS):
                        value_events(AT, q, group, 0)
                for n in range(AT.quad_tiles(last) - 4, AT.quad_tiles(last)):
                    split_hi(AT, q, n, last)
            quads(act, at_body)

            act.wait_ge(fin_T, FIRST_HALVES)
            for t in range(ST):
                nc.scalar.activation(raw[:, t, 0:S], final_bank(t, 0)[:, :], ACT.Square,
                                     accum_out=cols[:, t:t + 1]).then_inc(fin_sq, 1)
            act.wait_ge(fin_base, 1)
            for t in range(ST):
                act.wait_ge(fin_T, second_half(t))
                nc.scalar.activation(raw[:, t, S:2 * S], final_bank(t, 1)[:, :], ACT.Square,
                                     accum_out=cols[:, 4 + t:5 + t]).then_inc(fin_sq, 1)
                act.wait_ge(fin_sq, ST + t + 1)
                nc.scalar.activation(cols[:, 8 + t:9 + t], cols[:, 4 + t:5 + t], ACT.Ln, scale=1.0 / D,
                                     bias=cols[:, t:t + 1]).then_inc(fin_step, 1)
                act.wait_ge(fin_step, t + 1)
                nc.scalar.activation(cols[:, 12 + t:13 + t], cols[:, 8 + t:9 + t], ACT.Exp, scale=-0.5).then_inc(fin_rstd, 1)

        @block.vector
        def _(dve):
            def split_lo(layer, q, n, last):
                if layer is AT and last and n + SLOTS >= layer.quad_tiles(True):
                    return
                number, slot, _ = layer.tile(q, n)
                dve.wait_ge(hi_ready, number + SLOTS + 1)
                nc.vector.tensor_tensor(w["lo"][:, slot, :], raw[:, slot, :], w["hi"][:, slot, :].bitcast(F32),
                                        ALU.subtract).then_inc(w_ready, 1)

            def first_lo(n):
                dve.wait_ge(hi_ready, n + 1)
                nc.vector.tensor_tensor(w["lo"][:, n, :], raw[:, n, :], w["hi"][:, n, :].bitcast(F32),
                                        ALU.subtract).then_inc(w_ready, 1)

            def norm(which):
                dve.wait_ge(rstd_ready, which + 1)
                for k in range(KT + 1):
                    if k < KT:
                        if k >= 2:
                            dve.wait_ge(u_ready, which * KT + k - 1)
                        nc.vector.scalar_tensor_tensor(out=tmp[:, k % 2, :], in0=hT[:, k, :],
                                                       scalar=param[:, 64 + which * KT + k:65 + which * KT + k],
                                                       in1=rstd[:, :], op0=ALU.mult, op1=ALU.mult).then_inc(u_made, 1)
                    if k:
                        dve.wait_ge(u_hi_ready, which * KT + k)
                        nc.vector.tensor_tensor(u["lo"][:, k - 1, :], tmp[:, (k - 1) % 2, :],
                                                u["hi"][:, k - 1, :].bitcast(F32), ALU.subtract).then_inc(u_ready, 1)
                    if which == 0 and k in (2, 4, 6):
                        first_lo(k // 2)
                    elif which == 1 and k in (2, 4):
                        split_lo(HG, NQ - 1, HG.quad_tiles(True) - 3 + k // 2, True)

            nc.vector.memset(eps[:, :], EPS).then_inc(eps_ready, 1)
            for i in range(2 * ST):
                t, half = i // 2, i % 2
                if i == 2 * ST - 1:
                    dve.wait_ge(x_rstd, 1)
                    nc.vector.tensor_tensor(y_f[:, :].rearrange("p (t n) -> p t n", t=ST),
                                            ident[:, :].unsqueeze(1).broadcast_to([P, ST, P]),
                                            cols[:, 8:12].unsqueeze(2).broadcast_to([P, ST, P]), ALU.mult)\
                        .then_inc(diag_ready, 1)
                dve.wait_ge(x_T, 4 * i + 4)
                nc.vector.tensor_copy(hT[:, 4 * half:4 * half + 4, t * P:(t + 1) * P],
                                      inner[i % 4][:, :].rearrange("p (a b) -> p a b", b=P)).then_inc(x_copied, 1)
            dve.wait_ge(param_T, 1)
            nc.vector.tensor_copy(param[:, :], proj[0][:, 0:80]).then_inc(param_ready, 1)
            first_lo(0)
            dve.wait_ge(param_ready, 1)
            norm(0)
            nc.vector.tensor_tensor(lb[:, :], param[:, 0:H], param[:, H:2 * H], ALU.max).then_inc(lb_step, 1)
            dve.wait_ge(lb_step, 1)
            nc.vector.tensor_tensor(oml[:, :], lb[:, :], param[:, 2 * H:3 * H], ALU.max).then_inc(lb_step, 1)
            dve.wait_ge(lb_step, 2)
            for r in range(3):
                ins = nc.vector.tensor_tensor(param[:, r * H:(r + 1) * H], param[:, r * H:(r + 1) * H],
                                              oml[:, :], ALU.subtract)
            ins.then_inc(lb_step, 1)
            dve.wait_ge(lb_exp, 1)
            steps = 3

            def step(ins):
                nonlocal steps
                steps += 1
                ins.then_inc(lb_step, 1)
                dve.wait_ge(lb_step, steps)

            step(nc.vector.tensor_tensor(lb[:, :], param[:, 0:H], param[:, H:2 * H], ALU.add))
            step(nc.vector.tensor_tensor(oml[:, :], lb[:, :], param[:, 2 * H:3 * H], ALU.add))
            step(nc.vector.reciprocal(oml[:, :], oml[:, :]))
            step(nc.vector.tensor_tensor(lb[:, :], param[:, 0:H], oml[:, :], ALU.mult))
            step(nc.vector.tensor_scalar(oml[:, :], lb[:, :], -1.0, 1.0, ALU.mult, ALU.add))
            dve.wait_ge(const_loaded[6], 16)
            for g in range(GROUPS):
                dve.wait_ge(ext_done, g + 1)
                nc.vector.tensor_tensor(ext_sb[:, g * EXT:(g + 1) * EXT], inner[1 + g][0:H, 0:EXT],
                                        relmask_sb[:, g * EXT:(g + 1) * EXT], ALU.add).then_inc(ext_ready, 1)
            for n in range(3):
                split_lo(HG, None, n, False)
            step(nc.vector.memset(sT[:, :], 0.0))
            step(nc.vector.memset(dec[:, :, :], 1.0))
            dve.wait_ge(const_loaded[4], 32)
            dve.wait_ge(ext_stored, 16)
            split_lo(HG, None, 3, False)

            def gate(layer, q, h, g, event):
                _, bank, _ = layer.event(q, event)
                dve.wait_ge(sigma_ready, g + 1)
                nc.vector.tensor_tensor(sg[:, :], proj[bank][:, :], eg[:, :], ALU.mult).then_inc(bank_free[bank], 1)

            def bound(t, signal):
                nc.vector.tensor_scalar(t[:, :], t[:, :], LN_MAX, None, ALU.min).then_inc(signal, 1)

            def bound_gate(g):
                dve.wait_ge(sigma_step, 2 * g + 1)
                bound(eg, sigma_bounded)

            def mask_scores(g):
                dve.wait_ge(scores_done, g + 1)
                blocks = lambda t: t.rearrange("p (b c) -> p b c", b=ST)
                for j in range(NC):
                    seen, chunk = (j + 1) * CH, slice(j * CH, (j + 1) * CH)
                    ins = nc.vector.tensor_tensor(blocks(sT[0:seen, :])[:, :, chunk], blocks(p_sc[0:seen, :])[:, :, chunk],
                                                  causal[0:seen, chunk].unsqueeze(1).broadcast_to([seen, ST, CH]), ALU.mult)
                ins.then_inc(sT_ready, 1)

            def states(link, g):
                dve.wait_ge(U_done, g + 1)
                link(nc.vector.tensor_copy(state[:, 0, :], p_U[:, 0:P]))
                link(nc.vector.scalar_tensor_tensor(out=state[:, 1, :], in0=state[:, 0, :], scalar=dec[:, 1, NC:NC + 1],
                                                    in1=p_U[:, P:2 * P], op0=ALU.mult, op1=ALU.add))
                nc.vector.scalar_tensor_tensor(out=state[:, 2, :], in0=state[:, 1, :], scalar=dec[:, 2, NC:NC + 1],
                                               in1=p_U[:, 2 * P:3 * P], op0=ALU.mult, op1=ALU.add)\
                    .then_inc(state_ready, 1)

            def forget(g):
                dve.wait_ge(sigf_ready, g + 1)
                nc.vector.tensor_scalar(fg[:, :], ef[:, :], oml[:, ds(g, 1)], lb[:, ds(g, 1)], ALU.mult, ALU.add)\
                    .then_inc(f_ready, 1)
                dve.wait_ge(f_ready, g + 1)
                nc.vector.tensor_scalar(kk[:, :], fg[:, :], -1.0, 1.0, ALU.mult, ALU.add)

            def cumulate(g):
                dve.wait_ge(lnf_ready, g + 1)
                nc.vector.tensor_tensor_scan(bb[:, :], restart[:, :], lnf[:, :], 0.0, ALU.mult, ALU.add)\
                    .then_inc(b_ready, 1)

            def decays(link, q, h, g, low_before):
                number, bank, _ = HG.event(q, 3 * h + Q_)
                chunk = lambda t: t[:, :].rearrange("p (b j c) -> p b j c", b=ST, j=NC)
                A = chunk(eb)[:, :, :, CH - 1:CH]
                dve.wait_ge(proj_done, number + 1)
                dve.wait_ge(eb_ready, 2 * g + 2)
                nc.vector.tensor_tensor(qd[:, :], proj[bank][:, :], eb[:, :], ALU.mult).then_inc(bank_free[bank], 1)
                flat = keys[:, :, :, :].rearrange("p b s k -> p b (s k)")
                own = bass.AP(flat.tensor, flat.offset, [list(flat.ap[0]), [(NC + 1) * P, ST], [P + CH, NC], [1, CH]])
                after = bass.AP(flat.tensor, flat.offset + P, [list(flat.ap[0]), [(NC + 1) * P, ST], [P + CH, NC], [1, CH]])
                link(nc.vector.tensor_tensor(own, chunk(kk), chunk(enb), ALU.mult))
                if low_before:
                    y_low(g - 1, h - 1)
                link(nc.vector.tensor_tensor(after, own, A.broadcast_to([P, ST, NC, CH]), ALU.mult))
                link(nc.vector.tensor_copy(dec[:, :, 1:2], A[:, :, 0, :]))
                for j in range(1, NC):
                    link(nc.vector.tensor_tensor(dec[:, :, j + 1:j + 2], dec[:, :, j:j + 1], A[:, :, j, :], ALU.mult))
                    ins = nc.vector.tensor_tensor(keys[:, :, j + 1, 0:j * CH], keys[:, :, j, 0:j * CH],
                                                  A[:, :, j, :].broadcast_to([P, ST, j * CH]), ALU.mult)
                    if j < NC - 1:
                        link(ins)
                    else:
                        ins.then_inc(keys_ready, 1)
                nc.vector.tensor_tensor(chunk(qs), chunk(qd), dec[:, :, 0:NC].unsqueeze(3).broadcast_to([P, ST, NC, CH]),
                                        ALU.mult).then_inc(q_ready, 1)

            def osq_low(g):
                dve.wait_ge(osq_hi_ready, g + 1)
                nc.vector.tensor_tensor(osq["lo"], enb[:, :], osq["hi"].bitcast(F32), ALU.subtract).then_inc(osq_ready, 1)

            def hg_output(link, g):
                dve.wait_ge(orstd_ready, g + 1)
                link(nc.vector.tensor_tensor(y_f[:, :], p_O[:, :], rstd[:, :], ALU.mult))
                nc.vector.scalar_tensor_tensor(out=y_f[:, :], in0=y_f[:, :], scalar=param[:, ds(g + 3 * H, 1)],
                                               in1=sg[:, :], op0=ALU.mult, op1=ALU.mult).then_inc(y_made, 1)

            def y_low(g, slot):
                dve.wait_ge(y_hi_ready, g + 1)
                nc.vector.tensor_tensor(y["lo"][:, slot, :], y_f[:, :], y["hi"][:, slot, :].bitcast(F32), ALU.subtract)\
                    .then_inc(y_ready, 1)

            def add_out(layer, q, event, k):
                number, bank, _ = layer.event(q, event)
                dve.wait_ge(proj_done, number + 1)
                nc.vector.tensor_tensor(hT[:, k, :], hT[:, k, :], proj[bank][:, :], ALU.add)\
                    .then_inc(bank_free[bank], 1)

            def out_shares(layer, q, last):
                tile = layer.heads + (0 if last else layer.pro)
                for i in range(4):
                    for c in (2 * i, 2 * i + 1):
                        add_out(layer, q, tile + c + (KT if last else 0), c)
                    if not (last and layer is HG):
                        split_lo(layer, q, tile + i, last)
                    elif i % 2:
                        split_lo(layer, q, tile + i // 2, last)

            def hg_body(q, last):
                links = 0

                def link(ins):
                    nonlocal links
                    links += 1
                    ins.then_inc(link_hg, 1)
                    dve.wait_ge(link_hg, q * LINKS_HG + links)

                for h in range(HQ):
                    g, before = head(q, h), head(q, h - 1) if h else None
                    if h:
                        gate(HG, q, h - 1, before, 3 * (h - 1) + G_)
                        mask_scores(before)
                    wait_emptied(dve, HG, q, 3 * h + F_)
                    bound(ef, sigf_bounded)
                    if h:
                        states(link, before)
                    forget(g)
                    cumulate(g)
                    split_lo(HG, q, 3 * h + F_, last)
                    if h:
                        osq_low(before)
                        hg_output(link, before)
                    early = last and h == HQ - 1
                    decays(link, q, h, g, early)
                    split_lo(HG, q, 3 * h + Q_, last)
                    if h and not early:
                        y_low(before, h - 1)
                    bound_gate(g)
                    split_lo(HG, q, 3 * h + G_, last)
                g = head(q, HQ - 1)
                gate(HG, q, HQ - 1, g, 3 * (HQ - 1) + G_)
                if last:
                    add_out(HG, q, HG.heads, 0)
                mask_scores(g)
                if last:
                    add_out(HG, q, HG.heads + 1, 1)
                states(link, g)
                if last:
                    add_out(HG, q, HG.heads + 2, 2)
                osq_low(g)
                if last:
                    add_out(HG, q, HG.heads + 3, 3)
                hg_output(link, g)
                y_low(g, HQ - 1)
                if last:
                    for k in range(4, KT):
                        add_out(HG, q, HG.heads + k, k)
                else:
                    for n in range(4):
                        split_lo(HG, q, HG.heads + n, last)
                out_shares(HG, q, last)
                assert links == LINKS_HG, links
            quads(dve, hg_body)

            norm(1)
            for n in range(AT.pro):
                split_lo(AT, None, n, False)

            def biases(g, first, tile, done, loaded_, banks, signal, link):
                dve.wait_ge(loaded_, 16 * g + 16)
                for i in range(2):
                    dve.wait_ge(done, 2 * g + i + 1)
                    if first == 0 and i == 0:
                        nc.vector.tensor_tensor(probs[:, 0, 0:P], banks[0][:, 0:P], tile[:, P:2 * P], ALU.add)
                        ins = nc.vector.tensor_tensor(probs[:, 1, :], banks[0][:, 2 * P:4 * P], tile, ALU.add)
                    else:
                        ins = nc.vector.tensor_tensor(probs[:, first + 2 * i:first + 2 * i + 2, :],
                                                      banks[i][:, :].rearrange("p (a b) -> p a b", a=2),
                                                      tile.unsqueeze(1).broadcast_to([P, 2, 2 * P]), ALU.add)
                ins.then_inc(bias_used, 1)
                dve.wait_ge(bias_used, 2 * g + (2 if first else 1))
                if first == 0:
                    nc.vector.tensor_reduce(stat[:, 0, 0, 0:1], probs[:, 0, 0:P], AX.X, ALU.max)
                    link(nc.vector.tensor_reduce(stat[:, 0, 0, 1:ST], probs[:, 1:ST, :], AX.X, ALU.max))
                else:
                    link(nc.vector.tensor_reduce(stat[:, 1, 0, :], probs[:, ST:2 * ST, :], AX.X, ALU.max))
                nc.vector.tensor_scalar(negm[:, first:first + ST], stat[:, first // ST, 0, :], -1.0, None, ALU.mult)\
                    .then_inc(signal, 1)

            def merge_and_scale(link, g):
                dve.wait_ge(stat_a, 32 * g + 32)
                dve.wait_ge(stat_b, 32 * g + 32)
                link(nc.vector.tensor_tensor(share[:, :, :], stat[:, :, 0, :], stat_o[:, :, 0, :], ALU.max))
                nc.vector.tensor_tensor(both[:, 0, :, :], stat[:, :, 0, :], share[:, :, :], ALU.subtract)
                nc.vector.tensor_tensor(both[:, 1, :, :], stat_o[:, :, 0, :], share[:, :, :], ALU.subtract)\
                    .then_inc(merge_in, 1)
                dve.wait_ge(merge_exp, g + 1)
                nc.vector.tensor_tensor(both[:, 0, :, :], merge[:, 0, :, :], stat[:, :, 1, :], ALU.mult)
                link(nc.vector.tensor_tensor(both[:, 1, :, :], merge[:, 1, :, :], stat_o[:, :, 1, :], ALU.mult))
                link(nc.vector.tensor_tensor(share[:, :, :], both[:, 0, :, :], both[:, 1, :, :], ALU.add))
                link(nc.vector.reciprocal(share[:, :, :], share[:, :, :]))
                link(nc.vector.tensor_tensor(share[:, :, :], share[:, :, :], merge[:, 0, :, :], ALU.mult))
                for i in range(2 * ST):
                    n = P if i == 0 else 2 * P
                    ins = nc.vector.tensor_scalar(probs[:, i, 0:n], probs[:, i, 0:n],
                                                  share[:, i // ST, i % ST:i % ST + 1], None, ALU.mult)
                    if i % ST == ST - 1:
                        ins.then_inc(scaled, 1)

            def copy_even(g, b):
                dve.wait_ge(T_done, 4 * g + b + 1)
                nc.vector.tensor_copy(pT[:, BATCHES[b][0]:BATCHES[b][-1] + 1, :],
                                      p_T[0][:, 0:len(BATCHES[b]) * P].rearrange("p (a b) -> p a b", b=P))\
                    .then_inc(T_even, 1)

            def at_output(g):
                dve.wait_ge(O_done, H + g + 1)
                nc.vector.tensor_tensor(y_f[:, :], p_O[:, :], sg[:, :], ALU.mult).then_inc(y_made, 1)

            def at_body(q, last):
                links = 0

                def link(ins):
                    nonlocal links
                    links += 1
                    ins.then_inc(link_at, 1)
                    dve.wait_ge(link_at, q * LINKS_AT + links)

                bias_r_flat = bias_r[:, :, :].rearrange("p a b -> p (a b)")
                for h in range(HQ):
                    g, before = head(q, h), head(q, h - 1) if h else None
                    for i in range(7):
                        if i == K1 and h:
                            at_output(before)
                            y_low(before + H, h - 1)
                        if i == K1:
                            biases(g, 0, bias_n[:, :], nat_done, bias_loaded[0], p_S, nat_logits, link)
                        if i == GA:
                            biases(g, ST, bias_r_flat, res_done, bias_loaded[1], p_S, res_logits, link)
                        if i == K0 and h:
                            merge_and_scale(link, before)
                        gate_first = last and h == HQ - 1
                        if i == GA and gate_first:
                            bound_gate(H + g)
                            gate(AT, q, h, H + g, 7 * h + GA)
                        split_lo(AT, q, 7 * h + i, last)
                        if i == GA and not gate_first:
                            bound_gate(H + g)
                            gate(AT, q, h, H + g, 7 * h + GA)
                        if i == K0 and h:
                            copy_even(before, 0)
                            copy_even(before, 2)
                g = head(q, HQ - 1)
                if last:
                    for k in range(3):
                        add_out(AT, q, AT.heads + k, k)
                merge_and_scale(link, g)
                if last:
                    add_out(AT, q, AT.heads + 3, 3)
                    add_out(AT, q, AT.heads + 4, 4)
                copy_even(g, 0)
                if last:
                    add_out(AT, q, AT.heads + 5, 5)
                copy_even(g, 2)
                if last:
                    add_out(AT, q, AT.heads + 6, 6)
                else:
                    split_lo(AT, q, AT.heads, last)
                at_output(g)
                y_low(g + H, HQ - 1)
                if last:
                    add_out(AT, q, AT.heads + 7, 7)
                else:
                    for n in range(1, AT.pro):
                        split_lo(AT, q, AT.heads + n, last)
                out_shares(AT, q, last)
                assert links == LINKS_AT, links
            quads(dve, at_body)

            dve.wait_ge(const_loaded[0], 32)
            dve.wait_ge(fin_sq, ST)
            nc.vector.tensor_scalar(cols[:, 0:ST], cols[:, 0:ST], 1.0 / D, EPS, ALU.mult, ALU.add).then_inc(fin_base, 1)
            for t in range(ST):
                dve.wait_ge(fin_rstd, t + 1)
                for i in range(2):
                    nc.vector.scalar_tensor_tensor(out=nat[t][:, i, :], in0=final_bank(t, i)[:, :],
                                                   scalar=cols[:, 12 + t:13 + t], in1=fg_bc[:, i * S:(i + 1) * S],
                                                   op0=ALU.mult, op1=ALU.mult).then_inc(fin_ready, 1)


def bucket_of(dist):
    exact = BUCKETS // 2
    df = np.maximum(dist, 1).astype(np.float32)
    octaves = np.log(df / np.float32(exact)) / np.float32(np.log(2048 / exact))
    large = exact + (octaves * np.float32(BUCKETS - exact)).astype(np.int32)
    return np.where(dist < exact, dist, np.minimum(large, BUCKETS - 1))


def shape_constants():
    consts = np.zeros((P, 2 * P + S), np.float32)
    consts[:, 0:P] = np.eye(P)
    consts[:, P:2 * P] = np.triu(np.ones((P, P)))
    consts[:, 2 * P:] = (np.arange(S) % CH != 0)
    onehot = np.zeros((BUCKETS, GROUPS, EXT), np.float32)
    relmask = np.full((H, GROUPS, EXT), MASKED, np.float32)
    for g, (window, dilation) in enumerate(((128, 1), (512, 4), (2048, 16))):
        order = 1 if g == 0 else RES
        for e in range(EXT):
            apart = 2 * P - 1 - e
            dist = apart * order
            if apart >= 0 and dist % dilation == 0 and dist <= window:
                onehot[bucket_of(np.array(dist)), g, e] = 1.0
                relmask[:, g, e] = 0.0
    return consts, onehot.reshape(BUCKETS, -1), relmask.reshape(H, -1)


def kernel(**inputs):
    import concourse.bacc as bacc
    from concourse.bass_utils import run_bass_kernel_spmd

    nc = bacc.Bacc("TRN2", target_bir_lowering=False, num_devices=1)
    consts, onehot, relmask = shape_constants()
    a = {n: np.ascontiguousarray(v) for n, v in inputs.items()}
    arrays = {
        "x": a["x"].reshape(S, D), "ln_g": a["ln_g"], "hg_w_in": a["hg_w_in"].reshape(D, -1),
        "hg_lb": a["hg_lb_logits"], "hg_norm": a["hg_norm_g"], "hg_w_out": a["hg_w_out"].reshape(W, D),
        "at_w_in": a["att_w_in"].reshape(D, -1), "at_w_out": a["att_w_out"].reshape(W, D),
        "rel_bias": a["rel_bias"], "final_g": a["final_g"], "consts": consts, "onehot": onehot, "relmask": relmask,
    }
    args = [nc.dram_tensor(n, v.shape, F32, kind="ExternalInput").ap() for n, v in arrays.items()]
    out = nc.dram_tensor("out", (S, D), F32, kind="ExternalOutput").ap()
    program(nc, *args, out)
    result = run_bass_kernel_spmd(nc, [arrays], core_ids=[0])
    return result.results[0]["out"].reshape(1, S, D)
```
